# Optimizing a Trainium2 kernel written in Bass

```python
import math
import jax, jax.numpy as jnp
from jax import lax
import numpy as np

D_MODEL = 2048
BATCH = 1
SEQ = 256
DEPTH = 1

DIFF_V_DIM = 128
DIFF_QK_DIM = 64
DIFF_WIDTH = D_MODEL // 2
DIFF_HEADS = DIFF_WIDTH // DIFF_V_DIM
FOX_HEAD_DIM = 128
FOX_WIDTH = D_MODEL // 2
FOX_HEADS = FOX_WIDTH // FOX_HEAD_DIM
ROPE_THETA = 500000.0
ROPE_DIM = DIFF_QK_DIM // 4
BLOCK_Q = 128
EPS = 1e-6

SPLIT_SIZES = (
    DIFF_HEADS * 2 * DIFF_QK_DIM,
    DIFF_HEADS * 2 * DIFF_QK_DIM,
    DIFF_WIDTH,
    DIFF_WIDTH,
    FOX_WIDTH,
    FOX_WIDTH,
    FOX_WIDTH,
    FOX_WIDTH,
    FOX_HEADS,
    D_MODEL,
    D_MODEL,
)
N_IN = sum(SPLIT_SIZES)

kernel_name = "hybrid_diffattn_fox_gated_block"

def rmsnorm(x, g):
    xf = x.astype(jnp.float32)
    y = xf * lax.rsqrt(jnp.mean(xf * xf, axis=-1, keepdims=True) + EPS)
    return (y * g.astype(jnp.float32)).astype(x.dtype)

def partial_rope(x, pos):
    half = ROPE_DIM // 2
    inv = ROPE_THETA ** (-jnp.arange(half, dtype=jnp.float32) * 2.0 / ROPE_DIM)
    ang = pos.astype(jnp.float32)[:, None] * inv[None, :]
    shape = (1, pos.shape[0]) + (1,) * (x.ndim - 3) + (half,)
    cos = jnp.cos(ang).reshape(shape).astype(x.dtype)
    sin = jnp.sin(ang).reshape(shape).astype(x.dtype)
    x1 = x[..., :half]
    x2 = x[..., half:ROPE_DIM]
    return jnp.concatenate([x1 * cos - x2 * sin, x2 * cos + x1 * sin, x[..., ROPE_DIM:]], axis=-1)

def causal_mask(q0, kend):
    qpos = jnp.arange(q0, q0 + BLOCK_Q)
    kpos = jnp.arange(kend)
    return qpos[:, None] >= kpos[None, :]

def diff_attention(q, k, v, lam):
    S = q.shape[1]
    scale = DIFF_QK_DIM ** -0.5
    outs = []
    for i in range(S // BLOCK_Q):
        q0, q1 = i * BLOCK_Q, (i + 1) * BLOCK_Q
        s = jnp.einsum('bqhmd,bkhmd->bhmqk', q[:, q0:q1], k[:, :q1]).astype(jnp.float32) * scale
        s = jnp.where(causal_mask(q0, q1), s, -jnp.inf)
        p = jax.nn.softmax(s, axis=-1)
        a = p[:, :, 0] - lam * p[:, :, 1]
        outs.append(jnp.einsum('bhqk,bkhd->bqhd', a.astype(v.dtype), v[:, :q1]))
    return jnp.concatenate(outs, axis=1)

def forgetting_attention(q, k, v, log_f):
    S = q.shape[1]
    scale = FOX_HEAD_DIM ** -0.5
    c = jnp.cumsum(log_f, axis=1).transpose(0, 2, 1)
    outs = []
    for i in range(S // BLOCK_Q):
        q0, q1 = i * BLOCK_Q, (i + 1) * BLOCK_Q
        s = jnp.einsum('bqhd,bkhd->bhqk', q[:, q0:q1], k[:, :q1]).astype(jnp.float32) * scale
        s = s + (c[:, :, q0:q1, None] - c[:, :, None, :q1])
        s = jnp.where(causal_mask(q0, q1), s, -jnp.inf)
        p = jax.nn.softmax(s, axis=-1)
        outs.append(jnp.einsum('bhqk,bkhd->bqhd', p.astype(v.dtype), v[:, :q1]))
    return jnp.concatenate(outs, axis=1)

def hybrid_mixer(h, w_in, lq1, lk1, lq2, lk2, g_subln, b_f, w_proj_a, w_proj_b, w_out, layer_idx):
    B, S, _ = h.shape
    pos = jnp.arange(S)
    z = jnp.einsum('bsd,dn->bsn', h, w_in)
    idx = np.cumsum(np.array(SPLIT_SIZES))[:-1].tolist()
    qa, ka, va, ga, qb, kb, vb, gb, fl, ma, mb = jnp.split(z, idx, axis=-1)

    qa = partial_rope(qa.reshape(B, S, DIFF_HEADS, 2, DIFF_QK_DIM), pos)
    ka = partial_rope(ka.reshape(B, S, DIFF_HEADS, 2, DIFF_QK_DIM), pos)
    va = va.reshape(B, S, DIFF_HEADS, DIFF_V_DIM)
    lam_init = 0.8 - 0.6 * math.exp(-0.3 * layer_idx)
    lam = (jnp.exp(jnp.sum(lq1.astype(jnp.float32) * lk1.astype(jnp.float32)))
           - jnp.exp(jnp.sum(lq2.astype(jnp.float32) * lk2.astype(jnp.float32))) + lam_init)
    oa = diff_attention(qa, ka, va, lam)
    oa = rmsnorm(oa, g_subln) * (1.0 - lam_init)
    oa = oa.reshape(B, S, DIFF_WIDTH) * jax.nn.silu(ga)
    ya = jnp.einsum('bsw,wd->bsd', oa, w_proj_a)

    log_f = jax.nn.log_sigmoid((fl + b_f).astype(jnp.float32))
    ob = forgetting_attention(qb.reshape(B, S, FOX_HEADS, FOX_HEAD_DIM),
                              kb.reshape(B, S, FOX_HEADS, FOX_HEAD_DIM),
                              vb.reshape(B, S, FOX_HEADS, FOX_HEAD_DIM), log_f)
    ob = ob.reshape(B, S, FOX_WIDTH) * jax.nn.silu(gb)
    yb = jnp.einsum('bsw,wd->bsd', ob, w_proj_b)

    m = jax.nn.sigmoid(ma) * ya + jax.nn.sigmoid(mb) * yb
    return jnp.einsum('bsd,de->bse', m, w_out)

def setup_inputs(seed: int = 0) -> dict:
    key = jax.random.key(seed)
    ks = jax.random.split(key, 14)
    f32 = jnp.float32
    x = jax.random.normal(ks[0], (BATCH, SEQ, D_MODEL), f32)
    g_norm = 1.0 + 0.02 * jax.random.normal(ks[1], (DEPTH, D_MODEL), f32)
    w_in = jax.random.normal(ks[2], (DEPTH, D_MODEL, N_IN), f32) * D_MODEL ** -0.5
    lambda_q1 = 0.1 * jax.random.normal(ks[3], (DEPTH, DIFF_QK_DIM), f32)
    lambda_k1 = 0.1 * jax.random.normal(ks[4], (DEPTH, DIFF_QK_DIM), f32)
    lambda_q2 = 0.1 * jax.random.normal(ks[5], (DEPTH, DIFF_QK_DIM), f32)
    lambda_k2 = 0.1 * jax.random.normal(ks[6], (DEPTH, DIFF_QK_DIM), f32)
    g_subln = 1.0 + 0.02 * jax.random.normal(ks[7], (DEPTH, DIFF_V_DIM), f32)
    b_forget = jax.random.uniform(ks[8], (DEPTH, FOX_HEADS), f32, minval=1.0, maxval=4.0)
    w_proj_a = jax.random.normal(ks[9], (DEPTH, DIFF_WIDTH, D_MODEL), f32) * DIFF_WIDTH ** -0.5
    w_proj_b = jax.random.normal(ks[10], (DEPTH, FOX_WIDTH, D_MODEL), f32) * FOX_WIDTH ** -0.5
    w_out = jax.random.normal(ks[11], (DEPTH, D_MODEL, D_MODEL), f32) * D_MODEL ** -0.5
    g_final = 1.0 + 0.02 * jax.random.normal(ks[12], (D_MODEL,), f32)
    return {"x": x, "g_norm": g_norm, "w_in": w_in,
            "lambda_q1": lambda_q1, "lambda_k1": lambda_k1,
            "lambda_q2": lambda_q2, "lambda_k2": lambda_k2,
            "g_subln": g_subln, "b_forget": b_forget,
            "w_proj_a": w_proj_a, "w_proj_b": w_proj_b, "w_out": w_out,
            "g_final": g_final}

def reference(x, g_norm, w_in, lambda_q1, lambda_k1, lambda_q2, lambda_k2, g_subln,
              b_forget, w_proj_a, w_proj_b, w_out, g_final):
    for l in range(DEPTH):
        h = rmsnorm(x, g_norm[l])
        x = x + hybrid_mixer(h, w_in[l], lambda_q1[l], lambda_k1[l], lambda_q2[l], lambda_k2[l],
                             g_subln[l], b_forget[l], w_proj_a[l], w_proj_b[l], w_out[l], l)
    return rmsnorm(x, g_final)


_drawn_inputs = setup_inputs


def setup_inputs(seed=0):
    import zlib

    import numpy as np

    out = dict(_drawn_inputs(seed))
    spreads = {}
    factors = {'g_norm': 4.816,
     'lambda_q1': 8.0,
     'lambda_k1': 5.904,
     'lambda_q2': 8.0,
     'lambda_k2': 2.718,
     'g_subln': 8.0,
     'g_final': 2.903}
    for name, (base, spread) in spreads.items():
        noise = np.random.default_rng([zlib.crc32(name.encode()), seed]).standard_normal(out[name].shape)
        drawn = base * np.exp(spread * noise) if base else spread * noise
        out[name] = __import__('jax').numpy.asarray(drawn.astype(out[name].dtype))
    for name, factor in factors.items():
        out[name] = (out[name] * factor).astype(out[name].dtype)
    return out
```

```python
import math

import numpy as np

import concourse.bass as bass
from concourse import mybir
from contextlib import ExitStack

P = 128
D_MODEL = 2048
SEQ = 256
M_TILES = SEQ // P
KT = D_MODEL // P
HEADS = 8
HD = 128
QK = 64
WIDTH = 1024
ROPE_HALF = 8
EPS = 1e-6
NEG = -3.0e38
LAM_INIT = 0.8 - 0.6 * math.exp(-0.3 * 0)
CHUNK = 512
RING = 4
TILES = 8
SPLIT_AHEAD = 4
DIFF_COL = 0
FOX_COL = 4 * WIDTH
FL_COL = 8 * WIDTH
MERGE_COL = FL_COL + HEADS
Q_OFF, K_OFF, V_OFF, G_OFF = 0, WIDTH, 2 * WIDTH, 3 * WIDTH
C_ZERO, C_MASK, C_TRI, C_COS, C_SIN, C_ALL = 0, P, 2 * P, 3 * P, 3 * P + 16, 3 * P + 32


def build(nc, x, g_norm, w_in, lq1, lk1, lq2, lk2, g_subln, b_forget, w_a, w_b, w_out, g_final,
          ident_in, consts_in, out):
    fp32 = mybir.dt.float32
    fp32r = mybir.dt.float32r
    ALU = mybir.AluOpType
    ACT = mybir.ActivationFunctionType
    AX = mybir.AxisListType
    ds = bass.ds

    w_in_v = w_in[0].rearrange("(k p) n -> p k n", p=P)
    w_a_v = w_a[0].rearrange("(k p) n -> p k n", p=P)
    w_b_v = w_b[0].rearrange("(k p) n -> p k n", p=P)
    w_out_v = w_out[0].rearrange("(k p) n -> p k n", p=P)
    x_v = x[0].rearrange("(m p) n -> p m n", p=P)
    out_v = out[0].rearrange("(m p) n -> p m n", p=P)
    c_rows_dram = nc.dram_tensor("c_rows_dram", [HEADS, SEQ], fp32, kind="Internal").ap()

    ctx = ExitStack()
    with ctx:
        def sb(name, shape, dt=fp32):
            return ctx.enter_context(nc.sbuf_tensor(name, shape, dt))

        def bank(name):
            return ctx.enter_context(nc.psum_tensor(name, [P, 512], fp32))

        def sem(name):
            return ctx.enter_context(nc.semaphore(name))

        w_raw = sb("w_raw", [P, RING, 2, CHUNK])
        w_hi = sb("w_hi", [P, RING, 2, CHUNK], fp32r)
        w_lo = sb("w_lo", [P, RING, 2, CHUNK], fp32r)
        hT_hi = sb("hT_hi", [P, KT, SEQ], fp32r)
        hT_lo = sb("hT_lo", [P, KT, SEQ], fp32r)
        fox_z = sb("fox_z", [P, M_TILES, 4 * WIDTH])
        diff_z = sb("diff_z", [P, M_TILES, 4 * WIDTH])
        oT_hi = sb("oT_hi", [P, 2 * HEADS, SEQ], fp32r)
        oT_lo = sb("oT_lo", [P, 2 * HEADS, SEQ], fp32r)
        rows = sb("rows", [P, HEADS * SEQ])
        ident = sb("ident", [P, P])
        consts = sb("consts", [P, C_ALL])
        gn_rows = sb("gn_rows", [KT, P])
        g_col = sb("g_col", [P, KT])
        gsub = sb("gsub", [P, HD])
        b_row = sb("b_row", [P, HEADS])
        lam_in = sb("lam_in", [P, 4, QK])
        lam_dot = sb("lam_dot", [P, 2])
        lam_exp = sb("lam_exp", [P, 2])
        lam_tmp = sb("lam_tmp", [P, 2, QK])
        neg_lam = sb("neg_lam", [P, 1])
        wfl = sb("wfl", [P, KT, HEADS])
        wfl_parts = sb("wfl_parts", [P, KT, 2 * HEADS], fp32r)
        ssq = sb("ssq", [P, M_TILES])
        ms = sb("ms", [P, M_TILES])
        neg_half = sb("neg_half", [P, M_TILES])
        rstd = sb("rstd", [P, M_TILES])
        fl = sb("fl", [P, M_TILES, HEADS])
        fl_lo = sb("fl_lo", [P, M_TILES, HEADS])
        fl_abs = sb("fl_abs", [P, M_TILES, HEADS])
        log_f = sb("log_f", [P, M_TILES, HEADS])
        c_nat = sb("c_nat", [P, M_TILES, HEADS])
        c_neg = sb("c_neg", [HEADS, SEQ])
        ones = sb("ones", [P, P])
        qk_nat = sb("qk_nat", [P, M_TILES, 2, HD])
        qkT = sb("qkT", [P, 2, SEQ])
        bias = sb("bias", [P, 3 * P])
        probs = sb("probs", [P, 2, 3 * P])
        wait_slot = sb("wait_slot", [P, 1])
        row_max = sb("row_max", [P, 4])
        neg_max = sb("neg_max", [P, 4])
        sums = sb("sums", [P, 4])
        inv = sb("inv", [P, 4])
        pT = sb("pT", [P, 3 * P])
        og = sb("og", [P, M_TILES, HD])
        o_ssq = sb("o_ssq", [P, M_TILES])
        o_ms = sb("o_ms", [P, M_TILES])
        o_rstd = sb("o_rstd", [P, M_TILES])
        junk = sb("junk", [P, M_TILES * P])
        y_ssq = sb("y_ssq", [P, M_TILES, 4])

        mask = consts[:, C_MASK:C_MASK + P]
        zero_mask = consts[:, C_ZERO:C_ZERO + 2 * P]
        tri = consts[:, C_TRI:C_TRI + P]
        cos = consts[:, C_COS:C_COS + 16].rearrange("p (m c) -> p m c", m=M_TILES)
        sin = consts[:, C_SIN:C_SIN + 16].rearrange("p (m c) -> p m c", m=M_TILES)
        x_sb = diff_z[:, 0, :].rearrange("p (m n) -> p m n", m=M_TILES)
        y_sb = diff_z[:, 1, :].rearrange("p (m n) -> p m n", m=M_TILES)
        m_a = diff_z[:, 1, 0:2 * CHUNK].rearrange("p (m n) -> p m n", m=M_TILES)
        m_b = diff_z[:, 1, 2 * CHUNK:4 * CHUNK].rearrange("p (m n) -> p m n", m=M_TILES)
        rope_t = fox_z[:, 0, 0:4 * 4 * HEADS * ROPE_HALF].rearrange("p (i b c) -> p i b c", i=4, c=ROPE_HALF)
        yg = fox_z[:, 0, :].rearrange("p (m n) -> p m n", m=M_TILES)
        square_out = fox_z[:, 1, :].rearrange("p (m n) -> p m n", m=M_TILES)

        Z = [bank(f"Z{i}") for i in range(4)]
        A, B, C, Dk = bank("A"), bank("B"), bank("C"), bank("Dk")
        T_BANKS = [A, B, C, Dk]

        SMALL = 16 * 7

        raw_loaded = [sem(f"raw_loaded{i}") for i in range(RING)]
        hi_ready, lo_ready, w_used = sem("hi_ready"), sem("lo_ready"), sem("w_used")
        evac = [sem("evac0"), sem("evac1")]
        x_loaded = [sem(f"x_loaded{i}") for i in range(4)]
        ident_loaded, gn_loaded, small_loaded = sem("ident_loaded"), sem("gn_loaded"), sem("small_loaded")
        wfl_loaded = sem("wfl_loaded")
        gT_done, g_col_ready = sem("gT_done"), sem("g_col_ready")
        xT_done, xh_ready, xl_ready = sem("xT_done"), sem("xh_ready"), sem("xl_ready")
        x_squared, ms_ready, rstd_ready = sem("x_squared"), sem("ms_ready"), sem("rstd_ready")
        pool_const = sem("pool_const")
        wfl_hi_ready, wfl_ready = sem("wfl_hi_ready"), sem("wfl_ready")
        fl_done, fl_ready, softplus_ready, log_f_ready = sem("fl_done"), sem("fl_ready"), sem("softplus_ready"), sem("log_f_ready")
        c_done, c_nat_ready, cT_done, c_neg_ready = sem("c_done"), sem("c_nat_ready"), sem("cT_done"), sem("c_neg_ready")
        c_stored, rows_loaded = sem("c_stored"), sem("rows_loaded")
        lam_dots, lam_exps, lam_ready = sem("lam_dots"), sem("lam_exps"), sem("lam_ready")
        act_step, dve_step, pool_step = sem("act_step"), sem("dve_step"), sem("pool_step")
        sig_done, gate_ready = sem("sig_done"), sem("gate_ready")
        qk_ready, bias_ready = sem("qk_ready"), sem("bias_ready")
        qkT_done, qkT_ready = sem("qkT_done"), sem("qkT_ready")
        scores_done, max_ready, exp_done, probs_ready = sem("scores_done"), sem("max_ready"), sem("exp_done"), sem("probs_ready")
        pT_done, pT_ready, o_done = sem("pT_done"), sem("pT_ready"), sem("o_done")
        o_ms_ready = sem("o_ms_ready")
        o_squared, o_rstd_ready, og_ready = sem("o_squared"), sem("o_rstd_ready"), sem("og_ready")
        oT_done, oT_hi_ready, oT_lo_ready = sem("oT_done"), sem("oT_hi_ready"), sem("oT_lo_ready")
        merge_sig, m_ready, mT_done = sem("merge_sig"), sem("m_ready"), sem("mT_done")
        mT_hi_ready, mT_lo_ready = sem("mT_hi_ready"), sem("mT_lo_ready")
        xres_loaded, gf_loaded = sem("xres_loaded"), sem("gf_loaded")
        y_squared, yg_ready = sem("y_squared"), sem("yg_ready")
        y_ms_ready, y_rstd_ready = sem("y_ms_ready"), sem("y_rstd_ready")
        out_ready, out_stored = [sem("out_ready0"), sem("out_ready1")], sem("out_stored")

        block = ctx.enter_context(nc.Block())

        @block.sync
        def _(sp):
            def load(c, j, src):
                if not (isinstance(c, int) and 8 * c + j < RING):
                    sp.wait_ge(lo_ready, 8 * c + (j - RING + 1))
                sp.dma_start(w_raw[:, j % RING], src).then_inc(raw_loaded[j % RING], 16)

            sp.dma_start(ident[:], ident_in).then_inc(ident_loaded, 16)
            sp.dma_start(gn_rows[:], g_norm[0].rearrange("(k p) -> k p", p=P)).then_inc(gn_loaded, 16)
            for j in range(TILES):
                load(0, j, w_in_v[:, 2 * j:2 * j + 2, FOX_COL:FOX_COL + CHUNK])
            with sp.Fori(1, 8) as c:
                for j in range(TILES):
                    load(c, j, w_in_v[:, 2 * j:2 * j + 2, ds(c * CHUNK + FOX_COL, CHUNK)])
            with sp.Fori(8, 16) as c:
                for j in range(TILES):
                    load(c, j, w_in_v[:, 2 * j:2 * j + 2, ds(c * CHUNK + (DIFF_COL - 8 * CHUNK), CHUNK)])
            with sp.Fori(16, 24) as c:
                for j in range(TILES):
                    load(c, j, w_in_v[:, 2 * j:2 * j + 2, ds(c * CHUNK + (MERGE_COL - 16 * CHUNK), CHUNK)])
            with sp.Fori(24, 28) as c:
                for j in range(TILES):
                    w = w_a_v if j < 4 else w_b_v
                    k = 2 * (j % 4)
                    load(c, j, w[:, k:k + 2, ds(c * CHUNK - 24 * CHUNK, CHUNK)])
            sp.wait_ge(oT_done, 2 * HEADS)
            sp.dma_start(x_sb, x_v).then_inc(xres_loaded, 16)
            sp.dma_start(rows[:], g_final.rearrange("(a n) -> a n", a=1).to_broadcast([P, D_MODEL])).then_inc(gf_loaded, 16)
            with sp.Fori(28, 32) as c:
                for j in range(TILES):
                    load(c, j, w_out_v[:, 2 * j:2 * j + 2, ds(c * CHUNK - 28 * CHUNK, CHUNK)])
            for h in range(2):
                sl = slice(h * 1024, (h + 1) * 1024)
                sp.wait_ge(out_ready[1], h + 1)
                sp.dma_start(out_v[:, 1, sl], yg[:, 1, sl]).then_inc(out_stored, 16)
            sp.wait_ge(out_stored, 4 * 16)

        @block.tensor
        def _(pe):
            def split_product(acc, a_hi, a_lo, slot, kk, first, last):
                pe.matmul(acc, a_hi, w_hi[:, slot, kk], start=first, stop=False)
                pe.matmul(acc, a_hi, w_lo[:, slot, kk], start=False, stop=False)
                return pe.matmul(acc, a_lo, w_hi[:, slot, kk], start=False, stop=last)

            def tile(c, j, pair, stat_hi, stat_lo, k0, first, last):
                pe.wait_ge(hi_ready, 8 * c + (j + 1))
                pe.wait_ge(lo_ready, 8 * c + (j + 1))
                for kk in range(2):
                    for m in range(M_TILES):
                        tok = slice(m * P, (m + 1) * P)
                        mm = split_product(Z[2 * pair + m][:], stat_hi[:, k0 + kk, tok], stat_lo[:, k0 + kk, tok],
                                           j % RING, kk, first and kk == 0, last and kk == 1)
                mm.then_inc(w_used, 1)

            def banks_free(fill):
                pe.wait_ge(evac[0], fill - 1)
                pe.wait_ge(evac[1], fill - 1)

            def z_tile(c, j, pair):
                tile(c, j, pair, hT_hi, hT_lo, 2 * j, j == 0, j == TILES - 1)

            def x_transposes(j):
                if j % 2 == 0:
                    pe.wait_ge(x_loaded[j // 2], 16)
                if j == 3:
                    pe.wait_ge(g_col_ready, 1)
                if j >= 4:
                    pe.wait_ge(xl_ready, j - 3)
                for kk in range(2):
                    for m in range(M_TILES):
                        k = 2 * j + kk
                        mm = pe.transpose(T_BANKS[j % 4][:, (2 * kk + m) * P:(2 * kk + m + 1) * P],
                                          x_sb[:, m, k * P:(k + 1) * P], ident[:])
                mm.then_inc(xT_done, 1)

            def head_transposes(g):
                pe.wait_ge(qk_ready, g + 1)
                for i in range(2):
                    for m in range(M_TILES):
                        mm = pe.transpose(A[:, (2 * i + m) * P:(2 * i + m + 1) * P], qk_nat[:, m, i, :], ident[:])
                mm.then_inc(qkT_done, 1)

            def scores(g, maps):
                pe.wait_ge(qkT_ready, g + 1)
                for i in range(maps):
                    part = slice(0, P) if maps == 1 else slice(i * QK, (i + 1) * QK)
                    S = (B, C)[i]
                    pe.matmul(S[:, 0:P], qkT[part, 0, 0:P], qkT[part, 1, 0:P], start=True, stop=True)
                    mm = pe.matmul(S[:, P:3 * P], qkT[part, 0, P:2 * P], qkT[part, 1, 0:2 * P], start=True, stop=True)
                mm.then_inc(scores_done, 1)

            def prob_transposes(ready, g):
                pe.wait_ge(ready[0], ready[1])
                for b in range(3):
                    mm = pe.transpose(Dk[:, b * P:(b + 1) * P], probs[:, 0, b * P:(b + 1) * P], ident[:])
                mm.then_inc(pT_done, 1)

            def values(g, v_z, h):
                pe.wait_ge(pT_ready, g + 1)
                col = h * HD + V_OFF
                pe.matmul(A[:, 0:P], pT[:, 0:P], v_z[:, 0, ds(col, HD)], start=True, stop=True)
                pe.matmul(A[:, P:2 * P], pT[:, P:2 * P], v_z[:, 0, ds(col, HD)], start=True, stop=False)
                pe.matmul(A[:, P:2 * P], pT[:, 2 * P:3 * P], v_z[:, 1, ds(col, HD)], start=False, stop=True).then_inc(o_done, 1)

            def gated_transposes(g):
                pe.wait_ge(og_ready, g + 1)
                for m in range(M_TILES):
                    mm = pe.transpose(Dk[:, m * P:(m + 1) * P], og[:, m, :], ident[:])
                mm.then_inc(oT_done, 1)

            def merged_transposes(n):
                pe.wait_ge(m_ready, n + 1)
                for i in range(4):
                    for m in range(M_TILES):
                        mm = pe.transpose((A, B)[i // 2][:, (2 * (i % 2) + m) * P:(2 * (i % 2) + m + 1) * P],
                                          m_a[:, m, i * P:(i + 1) * P], ident[:])
                mm.then_inc(mT_done, 1)

            pe.wait_ge(ident_loaded, 16)
            pe.wait_ge(gn_loaded, 16)
            pe.matmul(Dk[:, 0:KT], gn_rows[:, :], ident[0:KT, 0:KT], start=True, stop=True).then_inc(gT_done, 1)
            for j in range(4):
                x_transposes(j)
            for j in range(TILES):
                pe.wait_ge(xh_ready, j + 1)
                pe.wait_ge(xl_ready, j + 1)
                z_tile(0, j, 0)
                if j + 4 < TILES:
                    x_transposes(j + 4)
            pe.wait_ge(wfl_ready, 1)
            for m in range(M_TILES):
                for k in range(KT):
                    for n, part in enumerate((hT_hi, hT_lo)):
                        mm = pe.matmul(A[:, m * 2 * HEADS:(m + 1) * 2 * HEADS], part[:, k, m * P:(m + 1) * P],
                                       wfl_parts[:, k, :], start=(k == 0 and n == 0), stop=(k == KT - 1 and n == 1))
            mm.then_inc(fl_done, 1)
            for j in range(TILES):
                z_tile(1, j, 1)
                if j == 2:
                    pe.wait_ge(log_f_ready, 1)
                    pe.wait_ge(pool_const, 2)
                    pe.wait_ge(small_loaded, SMALL)
                    pe.matmul(B[:, 0:HEADS], tri, log_f[:, 0, :], start=True, stop=True)
                    pe.matmul(B[:, HEADS:2 * HEADS], ones[:], log_f[:, 0, :], start=True, stop=False)
                    pe.matmul(B[:, HEADS:2 * HEADS], tri, log_f[:, 1, :], start=False, stop=True).then_inc(c_done, 1)
                if j == 4:
                    pe.wait_ge(c_nat_ready, 1)
                    for m in range(M_TILES):
                        mm = pe.matmul(C[0:HEADS, m * P:(m + 1) * P], c_nat[:, m, :], ident[:], start=True, stop=True)
                    mm.then_inc(cT_done, 1)

            with pe.Fori(1, 4) as i:
                for half in range(2):
                    c = 2 * i + half
                    banks_free(c)
                    for j in range(TILES):
                        z_tile(c, j, half)
            with pe.Fori(4, 8) as i:
                for half in range(2):
                    c = 2 * i + half
                    banks_free(c)
                    for j in range(TILES):
                        z_tile(c, j, half)
                        if j == 0:
                            head_transposes(c - 8)
                        if j == 1:
                            scores(c - 8, 1)
                        if j == 4:
                            prob_transposes((exp_done, c - 7), c - 8)
                        if j == 5:
                            values(c - 8, fox_z, c - 8)
                        if j == 7:
                            gated_transposes(c - 8)
            with pe.Fori(8, 12) as i:
                for half in range(2):
                    c = 2 * i + half
                    banks_free(c)
                    for j in range(TILES):
                        z_tile(c, j, half)
                        if j == 0:
                            head_transposes(c - 8)
                        if j == 1:
                            scores(c - 8, 2)
                        if j == 4:
                            prob_transposes((probs_ready, c - 15), c - 8)
                        if j == 5:
                            values(c - 8, diff_z, c - 16)
                        if j == 7:
                            gated_transposes(c - 8)

            def projection(n):
                for j in range(TILES):
                    if j % 4 == 0:
                        banks_free(2 * n + (24 + j // 4))
                    if j < 4 and isinstance(n, int):
                        pe.wait_ge(oT_lo_ready, HEADS + 2 * j + 2)
                    tile(n + 24, j, j // 4, oT_hi, oT_lo, (HEADS if j < 4 else 0) + 2 * (j % 4), j % 4 == 0, j % 4 == 3)
                    if j == 1 and not isinstance(n, int):
                        merged_transposes(n - 1)

            projection(0)
            with pe.Fori(1, 4) as n:
                projection(n)
            for n in range(4):
                c = 28 + n
                banks_free(32 + n)
                for j in range(TILES):
                    if n == 0:
                        pe.wait_ge(mT_lo_ready, j + 1)
                    z_tile(c, j, n % 2)
                    if n == 0 and j == 1:
                        merged_transposes(3)

        @block.scalar
        def _(act):
            def split(c, j):
                act.wait_ge(w_used, 8 * c + (j + 1))
                act.wait_ge(raw_loaded[j % RING], 32 * c + (16 * (2 + (j >= 4))))
                act.activation(w_hi[:, j % RING], w_raw[:, j % RING], ACT.Copy).then_inc(hi_ready, 1)

            def evacuate(c, half, z, col):
                act.wait_ge(w_used, 8 * c + 8)
                act.activation(z[:, 0, ds(col, CHUNK)], Z[2 * half][:], ACT.Copy, scale=rstd[:, 0:1]).then_inc(evac[0], 1)

            def x_part(j):
                act.wait_ge(xT_done, j + 1)
                for kk in range(2):
                    k = 2 * j + kk
                    ins = act.activation(hT_hi[:, k, :], T_BANKS[j % 4][:, kk * SEQ:(kk + 1) * SEQ], ACT.Copy,
                                         scale=g_col[:, k:k + 1])
                ins.then_inc(xh_ready, 1)

            for i in range(4):
                act.dma_start(x_sb[:, :, i * 512:(i + 1) * 512], x_v[:, :, i * 512:(i + 1) * 512]).then_inc(x_loaded[i], 16)
            act.dma_start(consts[:], consts_in).then_inc(small_loaded, 16)
            act.dma_start(gsub[:], g_subln.to_broadcast([P, HD])).then_inc(small_loaded, 16)
            act.dma_start(b_row[:], b_forget.to_broadcast([P, HEADS])).then_inc(small_loaded, 16)
            for i, v in enumerate((lq1, lk1, lq2, lk2)):
                act.dma_start(lam_in[:, i, :], v.to_broadcast([P, QK])).then_inc(small_loaded, 16)
            act.dma_start(wfl[:], w_in_v[:, :, FL_COL:FL_COL + HEADS]).then_inc(wfl_loaded, 16)
            act.wait_ge(g_col_ready, 1)
            for j in range(RING):
                x_part(j)
                act.wait_ge(raw_loaded[j], 16)
                act.activation(w_hi[:, j], w_raw[:, j], ACT.Copy).then_inc(hi_ready, 1)
            for j in range(TILES):
                if j < 4:
                    x_part(j + 4)
                if j in (4, 5):
                    m = j - 4
                    act.activation(square_out[:, m, :], x_sb[:, m, :], ACT.Square, accum_out=ssq[:, m:m + 1]).then_inc(x_squared, 1)
                if j == 6:
                    act.wait_ge(wfl_loaded, 16)
                    act.activation(wfl_parts[:, :, 0:HEADS], wfl[:], ACT.Copy).then_inc(wfl_hi_ready, 1)
                split(0, j)
            act.wait_ge(rstd_ready, 1)
            evacuate(0, 0, fox_z, 0)
            for j in range(TILES):
                if j == 0:
                    act.wait_ge(fl_ready, 1)
                    act.activation(fl_abs[:], fl[:], ACT.Abs).then_inc(act_step, 1)
                    act.wait_ge(act_step, 1)
                    act.activation(fl_abs[:], fl_abs[:], ACT.Exp, scale=-1.0).then_inc(act_step, 1)
                    act.wait_ge(act_step, 2)
                    act.activation(fl_abs[:], fl_abs[:], ACT.Ln, bias=1.0).then_inc(softplus_ready, 1)
                if j == 6:
                    act.wait_ge(lam_dots, 2)
                    act.activation(lam_exp[:], lam_dot[:], ACT.Exp).then_inc(lam_exps, 1)
                split(1, j)
            evacuate(1, 1, fox_z, CHUNK)
            with act.Fori(1, 4) as i:
                for half in range(2):
                    c = 2 * i + half
                    for j in range(TILES):
                        split(c, j)
                    evacuate(c, half, fox_z, c * CHUNK)

            def gate_sigmoid(z, tmp, n):
                act.wait_ge(evac[0], n)
                act.wait_ge(evac[1], n)
                act.activation(tmp[:, :, G_OFF:G_OFF + WIDTH], z[:, :, G_OFF:G_OFF + WIDTH], ACT.Sigmoid).then_inc(sig_done, 1)

            def qkT_copy(g, q_scale):
                act.wait_ge(qkT_done, g + 1)
                act.activation(qkT[:, 0, :], A[:, 0:SEQ], ACT.Copy, scale=q_scale)
                act.activation(qkT[:, 1, :], A[:, SEQ:2 * SEQ], ACT.Copy).then_inc(qkT_ready, 1)

            def exps(g, maps, scale):
                act.wait_ge(max_ready, g + 1)
                for i in range(maps):
                    act.activation(probs[:, i, 0:P], probs[:, i, 0:P], ACT.Exp, bias=neg_max[:, 2 * i:2 * i + 1],
                                   scale=scale, accum_out=sums[:, 2 * i:2 * i + 1])
                    ins = act.activation(probs[:, i, P:3 * P], probs[:, i, P:3 * P], ACT.Exp,
                                         bias=neg_max[:, 2 * i + 1:2 * i + 2], scale=scale,
                                         accum_out=sums[:, 2 * i + 1:2 * i + 2])
                ins.then_inc(exp_done, 1)

            def gated_hi(g):
                act.wait_ge(oT_done, g + 1)
                act.activation(oT_hi[:, ds(g, 1), :], Dk[:, 0:SEQ].rearrange("p (a n) -> p a n", a=1), ACT.Copy).then_inc(oT_hi_ready, 1)

            gate_sigmoid(fox_z, diff_z, 8)
            with act.Fori(4, 8) as i:
                for half in range(2):
                    c = 2 * i + half
                    for j in range(TILES):
                        if j == 0:
                            qkT_copy(c - 8, HD ** -0.5)
                        if j == 1:
                            exps(c - 8, 1, 1.0)
                        if j == 7:
                            gated_hi(c - 8)
                        split(c, j)
                    evacuate(c, half, diff_z, c * CHUNK - 8 * CHUNK)
            gate_sigmoid(diff_z, fox_z, 16)
            with act.Fori(8, 12) as i:
                for half in range(2):
                    c = 2 * i + half
                    for j in range(TILES):
                        if j == 0:
                            qkT_copy(c - 8, 1.0)
                        if j == 1:
                            exps(c - 8, 2, QK ** -0.5)
                        if j == 5:
                            act.wait_ge(o_done, c - 7)
                            for m in range(M_TILES):
                                ins = act.activation(junk[:, m * P:(m + 1) * P], A[:, m * P:(m + 1) * P], ACT.Square,
                                                     accum_out=o_ssq[:, m:m + 1])
                            ins.then_inc(o_squared, 1)
                        if j == 7:
                            gated_hi(c - 8)
                        split(c, j)
                    evacuate(c, half, fox_z, c * CHUNK - 16 * CHUNK)

            def merged_hi(n):
                act.wait_ge(mT_done, n + 1)
                for b in range(2):
                    act.activation(hT_hi[:, ds(4 * n + 2 * b, 2), :], (A, B)[b][:].rearrange("p (a n) -> p a n", a=2),
                                   ACT.Copy).then_inc(mT_hi_ready, 1)

            def projection(n):
                for j in range(TILES):
                    if j < 2:
                        gate = fox_z[:, :, ds(n * CHUNK + j * D_MODEL, CHUNK)]
                        act.activation(gate, gate, ACT.Sigmoid).then_inc(merge_sig, 1)
                    if j == 2 and not isinstance(n, int):
                        merged_hi(n - 1)
                    split(n + 24, j)

            act.wait_ge(evac[1], 24)
            act.wait_ge(evac[0], 24)
            projection(0)
            with act.Fori(1, 4) as n:
                projection(n)
            for n in range(4):
                for j in range(TILES):
                    if n == 0 and j == 2:
                        merged_hi(3)
                    if 8 * (28 + n) + j + SPLIT_AHEAD < 256:
                        split(28 + n, j)
                for m in range(M_TILES):
                    act.wait_ge(evac[m], 33 + n)
                    act.activation(fox_z[:, 1, m * CHUNK:(m + 1) * CHUNK], y_sb[:, m, n * CHUNK:(n + 1) * CHUNK],
                                   ACT.Square, accum_out=y_ssq[:, m, n:n + 1]).then_inc(y_squared, 1)
            act.wait_ge(y_rstd_ready, 1)
            act.wait_ge(yg_ready, 8)
            for h in range(2):
                sl = slice(h * 1024, (h + 1) * 1024)
                act.activation(yg[:, 0, sl], yg[:, 0, sl], ACT.Copy, scale=rstd[:, 0:1]).then_inc(out_ready[0], 1)
            for h in range(2):
                sl = slice(h * 1024, (h + 1) * 1024)
                act.wait_ge(out_ready[0], h + 1)
                act.dma_start(out_v[:, 0, sl], yg[:, 0, sl]).then_inc(out_stored, 16)

        @block.vector
        def _(dve):
            step = [0]

            def chained(ins):
                step[0] += 1
                ins.then_inc(dve_step, 1)
                dve.wait_ge(dve_step, step[0])

            def split(c, j):
                dve.wait_ge(hi_ready, 8 * c + (j + 5))
                dve.tensor_tensor(w_lo[:, j % RING], w_raw[:, j % RING], w_hi[:, j % RING].bitcast(fp32),
                                  ALU.subtract).then_inc(lo_ready, 1)

            def evacuate(c, half, z, col):
                dve.wait_ge(w_used, 8 * c + 8)
                dve.tensor_scalar(z[:, 1, ds(col, CHUNK)], Z[2 * half + 1][:], rstd[:, 1:2], None,
                                  ALU.mult).then_inc(evac[1], 1)

            def x_part(j):
                dve.wait_ge(xh_ready, j + 1)
                for kk in range(2):
                    k = 2 * j + kk
                    ins = dve.scalar_tensor_tensor(hT_lo[:, k, :], T_BANKS[j % 4][:, kk * SEQ:(kk + 1) * SEQ],
                                                   g_col[:, k:k + 1], hT_hi[:, k, :].bitcast(fp32), ALU.mult, ALU.subtract)
                ins.then_inc(xl_ready, 1)

            dve.wait_ge(gT_done, 1)
            dve.tensor_copy(g_col[:], Dk[:, 0:KT]).then_inc(g_col_ready, 1)
            for j in range(RING):
                x_part(j)
                dve.wait_ge(hi_ready, j + 1)
                dve.tensor_tensor(w_lo[:, j], w_raw[:, j], w_hi[:, j].bitcast(fp32), ALU.subtract).then_inc(lo_ready, 1)
            for j in range(TILES):
                if j < 4:
                    x_part(j + 4)
                if j == 6:
                    dve.wait_ge(x_squared, 2)
                    dve.tensor_scalar(ms[:], ssq[:], 1.0 / D_MODEL, EPS, ALU.mult, ALU.add).then_inc(ms_ready, 1)
                if j == 7:
                    dve.wait_ge(wfl_hi_ready, 1)
                    dve.tensor_tensor(wfl_parts[:, :, HEADS:2 * HEADS], wfl[:], wfl_parts[:, :, 0:HEADS].bitcast(fp32),
                                      ALU.subtract).then_inc(wfl_ready, 1)
                split(0, j)
            dve.wait_ge(rstd_ready, 1)
            evacuate(0, 0, fox_z, 0)
            for j in range(TILES):
                if j == 0:
                    dve.wait_ge(fl_done, 1)
                    dve.wait_ge(small_loaded, SMALL)
                    for m in range(M_TILES):
                        c0 = m * 2 * HEADS
                        chained(dve.tensor_scalar(fl_lo[:, m, :], A[:, c0 + HEADS:c0 + 2 * HEADS], rstd[:, m:m + 1], None, ALU.mult))
                        chained(dve.scalar_tensor_tensor(fl[:, m, :], A[:, c0:c0 + HEADS], rstd[:, m:m + 1], fl_lo[:, m, :],
                                                         ALU.mult, ALU.add))
                    dve.tensor_tensor(fl[:], fl[:], b_row[:].unsqueeze(1).to_broadcast([P, M_TILES, HEADS]),
                                      ALU.add).then_inc(fl_ready, 1)
                if j == 1:
                    dve.wait_ge(softplus_ready, 1)
                    dve.scalar_tensor_tensor(log_f[:], fl[:], 0.0, fl_abs[:], ALU.min, ALU.subtract).then_inc(log_f_ready, 1)
                if j == 2:
                    dve.wait_ge(c_done, 1)
                    dve.tensor_copy(c_nat[:].rearrange("p m h -> p (m h)"), B[:, 0:2 * HEADS]).then_inc(c_nat_ready, 1)
                if j == 4:
                    dve.wait_ge(cT_done, 1)
                    dve.tensor_scalar(c_neg[:], C[0:HEADS, 0:SEQ], -1.0, None, ALU.mult).then_inc(c_neg_ready, 1)
                if j == 5:
                    for i in range(2):
                        dve.tensor_tensor_reduce(lam_tmp[:, i], lam_in[:, 2 * i, :], lam_in[:, 2 * i + 1, :], 1.0, 0.0,
                                                 ALU.mult, ALU.add, lam_dot[:, i:i + 1]).then_inc(lam_dots, 1)
                if j == 7:
                    dve.wait_ge(lam_exps, 1)
                    chained(dve.tensor_tensor(neg_lam[:], lam_exp[:, 1:2], lam_exp[:, 0:1], ALU.subtract))
                    dve.tensor_scalar(neg_lam[:], neg_lam[:], -LAM_INIT, None, ALU.add).then_inc(lam_ready, 1)
                split(1, j)
            evacuate(1, 1, fox_z, CHUNK)
            with dve.Fori(1, 4) as i:
                for half in range(2):
                    c = 2 * i + half
                    for j in range(TILES):
                        split(c, j)
                    evacuate(c, half, fox_z, c * CHUNK)

            def masked_max(S, i, add0, add1):
                if i == 0:
                    dve.memset(wait_slot[:], 0.0)
                dve.tensor_tensor_reduce(probs[:, i, 0:P], S[:, 0:P], add0, 1.0, NEG, ALU.add, ALU.max,
                                         row_max[:, 2 * i:2 * i + 1]).then_inc(dve_step, 1)
                dve.tensor_tensor_reduce(probs[:, i, P:3 * P], S[:, P:3 * P], add1, 1.0, NEG, ALU.add, ALU.max,
                                         row_max[:, 2 * i + 1:2 * i + 2]).then_inc(dve_step, 1)

            def gated_lo(g):
                dve.wait_ge(oT_hi_ready, g + 1)
                dve.tensor_tensor(oT_lo[:, ds(g, 1), :], Dk[:, 0:SEQ].rearrange("p (a n) -> p a n", a=1),
                                  oT_hi[:, ds(g, 1), :].bitcast(fp32), ALU.subtract).then_inc(oT_lo_ready, 1)

            def pT_copy(g):
                dve.wait_ge(pT_done, g + 1)
                dve.tensor_copy(pT[:], Dk[:, 0:3 * P]).then_inc(pT_ready, 1)

            s0 = step[0]
            with dve.Fori(4, 8) as i:
                for half in range(2):
                    c = 2 * i + half
                    for j in range(TILES):
                        if j == 1:
                            dve.wait_ge(scores_done, c - 7)
                            dve.wait_ge(bias_ready, 2 * c - 14)
                            masked_max(B, 0, bias[:, 0:P], bias[:, P:3 * P])
                            dve.wait_ge(dve_step, 2 * c + (s0 + 2 - 16))
                            dve.tensor_scalar(neg_max[:, 0:2], row_max[:, 0:2], -1.0, None, ALU.mult).then_inc(max_ready, 1)
                        if j == 3:
                            dve.wait_ge(exp_done, c - 7)
                            dve.reciprocal(inv[:, 0:2], sums[:, 0:2])
                        if j == 4:
                            pT_copy(c - 8)
                        if j == 5:
                            dve.wait_ge(o_done, c - 7)
                            dve.wait_ge(gate_ready, 1)
                            for m in range(M_TILES):
                                ins = dve.scalar_tensor_tensor(og[:, m, :], A[:, m * P:(m + 1) * P], inv[:, m:m + 1],
                                                               fox_z[:, m, ds(c * HD + (G_OFF - 8 * HD), HD)],
                                                               ALU.mult, ALU.mult)
                            ins.then_inc(og_ready, 1)
                        if j == 7:
                            gated_lo(c - 8)
                        split(c, j)
                    evacuate(c, half, diff_z, c * CHUNK - 8 * CHUNK)
            s1 = s0 + 16
            with dve.Fori(8, 12) as i:
                for half in range(2):
                    c = 2 * i + half
                    for j in range(TILES):
                        if j == 1:
                            dve.wait_ge(scores_done, c - 7)
                            for mp, S in enumerate((B, C)):
                                masked_max(S, mp, mask, zero_mask)
                            dve.wait_ge(dve_step, 8 * c + (s1 + 4 - 128))
                            dve.tensor_scalar(neg_max[:], row_max[:], -(QK ** -0.5), None, ALU.mult).then_inc(max_ready, 1)
                        if j == 2:
                            dve.wait_ge(exp_done, c - 7)
                            dve.reciprocal(inv[:], sums[:]).then_inc(dve_step, 1)
                            dve.wait_ge(dve_step, 8 * c + (s1 + 5 - 128))
                            dve.tensor_scalar(inv[:, 2:4], inv[:, 2:4], neg_lam[:, 0:1], None, ALU.mult).then_inc(dve_step, 1)
                            dve.wait_ge(dve_step, 8 * c + (s1 + 6 - 128))
                            for m, sl in enumerate((slice(0, P), slice(P, 3 * P))):
                                dve.tensor_scalar(probs[:, 1, sl], probs[:, 1, sl], inv[:, 2 + m:3 + m], None,
                                                  ALU.mult).then_inc(dve_step, 1)
                            dve.wait_ge(dve_step, 8 * c + (s1 + 8 - 128))
                            for m, sl in enumerate((slice(0, P), slice(P, 3 * P))):
                                ins = dve.scalar_tensor_tensor(probs[:, 0, sl], probs[:, 0, sl], inv[:, m:m + 1],
                                                               probs[:, 1, sl], ALU.mult, ALU.add)
                            ins.then_inc(probs_ready, 1)
                        if j == 4:
                            pT_copy(c - 8)
                        if j == 6:
                            dve.wait_ge(o_squared, c - 15)
                            dve.tensor_scalar(o_ms[:], o_ssq[:], 1.0 / HD, EPS, ALU.mult, ALU.add).then_inc(o_ms_ready, 1)
                            split(c, j)
                            dve.wait_ge(o_rstd_ready, c - 15)
                            dve.wait_ge(gate_ready, 3)
                            for m in range(M_TILES):
                                ins = dve.scalar_tensor_tensor(og[:, m, :], A[:, m * P:(m + 1) * P], o_rstd[:, m:m + 1],
                                                               diff_z[:, m, ds(c * HD + (G_OFF - 16 * HD), HD)],
                                                               ALU.mult, ALU.mult)
                            ins.then_inc(og_ready, 1)
                        if j == 7:
                            gated_lo(c - 8)
                        if j != 6:
                            split(c, j)
                    evacuate(c, half, fox_z, c * CHUNK - 16 * CHUNK)

            def merged_lo(n):
                for b in range(2):
                    dve.wait_ge(mT_hi_ready, 2 * n + (b + 1))
                    dve.tensor_tensor(hT_lo[:, ds(4 * n + 2 * b, 2), :], (A, B)[b][:].rearrange("p (a n) -> p a n", a=2),
                                      hT_hi[:, ds(4 * n + 2 * b, 2), :].bitcast(fp32), ALU.subtract).then_inc(mT_lo_ready, 1)

            def gate_branch(n, branch, dst):
                dve.wait_ge(w_used, 8 * n + (8 * 24 + 4 + 4 * branch))
                dve.wait_ge(merge_sig, 2 * n + (1 + branch))
                for m in range(M_TILES):
                    dve.tensor_tensor(dst[:, m, :], Z[2 * branch + m][:],
                                      fox_z[:, m, ds(n * CHUNK + branch * D_MODEL, CHUNK)], ALU.mult).then_inc(evac[m], 1)

            def projection(n):
                for j in range(TILES):
                    if j == 2 and not isinstance(n, int):
                        merged_lo(n - 1)
                    split(n + 24, j)
                    if j == 3:
                        gate_branch(n, 0, m_a)
                gate_branch(n, 1, m_b)
                dve.wait_ge(evac[1], 2 * n + 26)
                dve.tensor_tensor(m_a, m_a, m_b, ALU.add).then_inc(m_ready, 1)

            projection(0)
            with dve.Fori(1, 4) as n:
                projection(n)
            dve.wait_ge(xres_loaded, 16)
            for n in range(4):
                for j in range(TILES):
                    if n == 0 and j == 2:
                        merged_lo(3)
                    if 8 * (28 + n) + j + SPLIT_AHEAD < 256:
                        split(28 + n, j)
                dve.wait_ge(w_used, 8 * (29 + n))
                for m in range(M_TILES):
                    sl = slice(n * CHUNK, (n + 1) * CHUNK)
                    dve.tensor_tensor(y_sb[:, m, sl], Z[2 * (n % 2) + m][:], x_sb[:, m, sl],
                                      ALU.add).then_inc(evac[m], 1)
            dve.wait_ge(y_squared, 8)
            dve.tensor_reduce(ssq[:], y_ssq[:], AX.X, ALU.add).then_inc(y_ms_ready, 1)
            dve.wait_ge(y_ms_ready, 1)
            dve.tensor_scalar(ms[:], ssq[:], 1.0 / D_MODEL, EPS, ALU.mult, ALU.add).then_inc(y_ms_ready, 1)
            dve.wait_ge(y_rstd_ready, 1)
            dve.wait_ge(yg_ready, 8)
            for h in range(2):
                sl = slice(h * 1024, (h + 1) * 1024)
                dve.tensor_scalar(yg[:, 1, sl], yg[:, 1, sl], rstd[:, 1:2], None, ALU.mult).then_inc(out_ready[1], 1)

        @block.gpsimd
        def _(pool):
            step = [0]

            def chained(ins):
                step[0] += 1
                ins.then_inc(pool_step, 1)
                pool.wait_ge(pool_step, step[0])

            pool.memset(ones[:], 1.0).then_inc(pool_const, 1)
            pool.memset(neg_half[:], -0.5).then_inc(pool_const, 1)
            pool.wait_ge(pool_const, 2)
            pool.wait_ge(small_loaded, SMALL)
            pool.tensor_scalar(gsub[:], gsub[:], 1.0 - LAM_INIT, None, ALU.mult).then_inc(pool_const, 1)
            pool.wait_ge(ms_ready, 1)
            pool.tensor_tensor(rstd[:], ms[:], neg_half[:], ALU.pow).then_inc(rstd_ready, 1)
            pool.wait_ge(c_neg_ready, 1)
            pool.dma_start(c_rows_dram, c_neg[:]).then_inc(c_stored, 16)
            pool.wait_ge(c_stored, 16)
            pool.dma_start(rows[:], c_rows_dram.rearrange("(a h) n -> a (h n)", a=1).to_broadcast([P, HEADS * SEQ])).then_inc(rows_loaded, 16)

            def past(c):
                pool.wait_ge(w_used, 8 * c - 2)

            def head_copy(z, h):
                src = z[:, :, 0:2 * WIDTH].rearrange("p m (i n) -> p m i n", i=2)[:, :, :, ds(h * HD, HD)]
                pool.tensor_copy(qk_nat[:], src).then_inc(qk_ready, 1)

            def head_bias(h, steps):
                for m, sl in enumerate((slice(0, P), slice(P, 3 * P))):
                    n = (m + 1) * P
                    pool.tensor_tensor(bias[:, sl], rows[:].rearrange("p (h n) -> p h n", h=HEADS)[:, ds(h, 1), 0:n],
                                       c_nat[:, m, ds(h, 1)].unsqueeze(2).to_broadcast([P, 1, n]),
                                       ALU.add).then_inc(pool_step, 1)
                pool.wait_ge(pool_step, steps)
                for sl in (slice(0, P), slice(2 * P, 3 * P)):
                    pool.tensor_tensor(bias[:, sl], bias[:, sl], mask, ALU.add).then_inc(bias_ready, 1)

            def q_k_ready(n):
                pool.wait_ge(evac[0], n)
                pool.wait_ge(evac[1], n)

            q_k_ready(4)
            pool.wait_ge(rows_loaded, 16)
            pool.wait_ge(c_nat_ready, 1)
            head_copy(fox_z, 0)
            head_bias(0, step[0] + 2)
            pool.wait_ge(sig_done, 1)
            gate = fox_z[:, :, G_OFF:G_OFF + WIDTH]
            pool.tensor_tensor(gate, gate, diff_z[:, :, G_OFF:G_OFF + WIDTH], ALU.mult).then_inc(gate_ready, 1)
            with pool.Fori(9, 16) as c:
                past(c)
                head_copy(fox_z, c - 8)
                head_bias(c - 8, 2 * c + (step[0] + 2 - 16))
            step[0] += 2 * HEADS

            q_k_ready(12)
            for m in range(M_TILES):
                blocks = diff_z[:, m, 0:2 * WIDTH].rearrange("p (b d) -> p b d", d=QK)
                x1, x2 = blocks[:, :, 0:ROPE_HALF], blocks[:, :, ROPE_HALF:2 * ROPE_HALF]
                shape = [P, 2 * 2 * HEADS, ROPE_HALF]
                cos_m, sin_m = (t[:, m, :].unsqueeze(1).to_broadcast(shape) for t in (cos, sin))
                for i, (u, v) in enumerate(((x1, cos_m), (x2, sin_m), (x2, cos_m), (x1, sin_m))):
                    ins = pool.tensor_tensor(rope_t[:, i], u, v, ALU.mult)
                chained(ins)
                pool.tensor_tensor(x1, rope_t[:, 0], rope_t[:, 1], ALU.subtract)
                chained(pool.tensor_tensor(x2, rope_t[:, 2], rope_t[:, 3], ALU.add))
            past(16)
            head_copy(diff_z, 0)
            pool.wait_ge(sig_done, 2)
            gate = diff_z[:, :, G_OFF:G_OFF + WIDTH]
            chained(pool.tensor_tensor(gate, gate, fox_z[:, :, G_OFF:G_OFF + WIDTH], ALU.mult))
            pool.wait_ge(pool_const, 3)
            for m in range(M_TILES):
                gate = diff_z[:, m, G_OFF:G_OFF + WIDTH].rearrange("p (h d) -> p h d", d=HD)
                pool.tensor_tensor(gate, gate, gsub[:].unsqueeze(1).to_broadcast([P, HEADS, HD]),
                                   ALU.mult).then_inc(gate_ready, 1)
            def head_rstd(c):
                pool.wait_ge(o_ms_ready, c - 15)
                pool.tensor_tensor(o_rstd[:], o_ms[:], neg_half[:], ALU.pow).then_inc(o_rstd_ready, 1)

            with pool.Fori(16, 23) as c:
                head_rstd(c)
                past(c + 1)
                head_copy(diff_z, c - 15)
            head_rstd(23)

            pool.wait_ge(gf_loaded, 16)
            for n in range(4):
                sl = slice(n * CHUNK, (n + 1) * CHUNK)
                for m in range(M_TILES):
                    pool.wait_ge(evac[m], 33 + n)
                    pool.tensor_tensor(yg[:, m, sl], y_sb[:, m, sl], rows[:, sl], ALU.mult).then_inc(yg_ready, 1)
            pool.wait_ge(y_ms_ready, 2)
            pool.tensor_tensor(rstd[:], ms[:], neg_half[:], ALU.pow).then_inc(y_rstd_ready, 1)


def kernel(x, g_norm, w_in, lambda_q1, lambda_k1, lambda_q2, lambda_k2, g_subln, b_forget,
           w_proj_a, w_proj_b, w_out, g_final):
    import concourse.bacc as bacc
    from concourse.bass_utils import run_bass_kernel_spmd

    pos = np.arange(SEQ, dtype=np.float32)
    inv_freq = np.float32(500000.0) ** (-np.arange(ROPE_HALF, dtype=np.float32) * 2.0 / (2 * ROPE_HALF))
    angle = (pos[:, None] * inv_freq[None, :].astype(np.float32)).reshape(M_TILES, P, ROPE_HALF).transpose(1, 0, 2)
    i = np.arange(P)
    consts = np.zeros((P, C_ALL), np.float32)
    consts[:, C_MASK:C_MASK + P] = np.where(i[:, None] >= i[None, :], 0.0, NEG)
    consts[:, C_TRI:C_TRI + P] = i[:, None] <= i[None, :]
    consts[:, C_COS:C_COS + 16] = np.cos(angle).reshape(P, 16)
    consts[:, C_SIN:C_SIN + 16] = np.sin(angle).reshape(P, 16)

    named = dict(x=x, g_norm=g_norm, w_in=w_in, lq1=lambda_q1, lk1=lambda_k1, lq2=lambda_q2, lk2=lambda_k2,
                 g_subln=g_subln, b_forget=b_forget, w_a=w_proj_a, w_b=w_proj_b, w_out=w_out, g_final=g_final,
                 ident=np.eye(P, dtype=np.float32), consts=consts)
    nc = bacc.Bacc("TRN2", target_bir_lowering=False, num_devices=1)
    arrays, args = {}, []
    for name, value in named.items():
        a = np.ascontiguousarray(value)
        arrays[f"in_{name}"] = a
        args.append(nc.dram_tensor(f"in_{name}", a.shape, mybir.dt.from_np(a.dtype), kind="ExternalInput").ap())
    args.append(nc.dram_tensor("out_y", (1, SEQ, D_MODEL), mybir.dt.float32, kind="ExternalOutput").ap())
    build(nc, *args)
    r = run_bass_kernel_spmd(nc, [arrays], core_ids=[0])
    return r.results[0]["out_y"]
```

```python
import math

import numpy as np

import concourse.bass as bass
from concourse import mybir
from contextlib import ExitStack

P = 128
D_MODEL = 2048
SEQ = 256
M_TILES = SEQ // P
KT = D_MODEL // P
HEADS = 8
HD = 128
QK = 64
WIDTH = 1024
ROPE_HALF = 8
EPS = 1e-6
NEG = -3.0e38
LAM_INIT = 0.8 - 0.6 * math.exp(-0.3 * 0)
CHUNK = 512
RING = 4
TILES = 8
SPLIT_AHEAD = 4
DIFF_COL = 0
FOX_COL = 4 * WIDTH
FL_COL = 8 * WIDTH
MERGE_COL = FL_COL + HEADS
Q_OFF, K_OFF, V_OFF, G_OFF = 0, WIDTH, 2 * WIDTH, 3 * WIDTH
C_ZERO, C_MASK, C_TRI, C_COS, C_SIN, C_SEL, C_ALL = 0, P, 2 * P, 3 * P, 3 * P + 16, 3 * P + 32, 3 * P + 40


def build(nc, x, g_norm, w_in, lq1, lk1, lq2, lk2, g_subln, b_forget, w_a, w_b, w_out, g_final,
          consts_in, out):
    fp32 = mybir.dt.float32
    fp32r = mybir.dt.float32r
    ALU = mybir.AluOpType
    ACT = mybir.ActivationFunctionType
    AX = mybir.AxisListType
    ds = bass.ds

    w_in_v = w_in[0].rearrange("(k p) n -> p k n", p=P)
    w_a_v = w_a[0].rearrange("(k p) n -> p k n", p=P)
    w_b_v = w_b[0].rearrange("(k p) n -> p k n", p=P)
    w_out_v = w_out[0].rearrange("(k p) n -> p k n", p=P)
    x_v = x[0].rearrange("(m p) n -> p m n", p=P)
    out_v = out[0].rearrange("(m p) n -> p m n", p=P)
    c_rows_dram = nc.dram_tensor("c_rows_dram", [HEADS, SEQ], fp32, kind="Internal").ap()

    ctx = ExitStack()
    with ctx:
        def sb(name, shape, dt=fp32):
            return ctx.enter_context(nc.sbuf_tensor(name, shape, dt))

        def bank(name):
            return ctx.enter_context(nc.psum_tensor(name, [P, 512], fp32))

        def sem(name):
            return ctx.enter_context(nc.semaphore(name))

        w_raw = sb("w_raw", [P, RING, 2, CHUNK])
        w_hi = sb("w_hi", [P, RING, 2, CHUNK], fp32r)
        w_lo = sb("w_lo", [P, RING, 2, CHUNK], fp32r)
        hT_hi = sb("hT_hi", [P, KT, SEQ], fp32r)
        hT_lo = sb("hT_lo", [P, KT, SEQ], fp32r)
        fox_z = sb("fox_z", [P, M_TILES, 4 * WIDTH])
        diff_z = sb("diff_z", [P, M_TILES, 4 * WIDTH])
        oT_hi = sb("oT_hi", [P, 2 * HEADS, SEQ], fp32r)
        oT_lo = sb("oT_lo", [P, 2 * HEADS, SEQ], fp32r)
        rows = sb("rows", [P, HEADS * SEQ])
        ident = sb("ident", [P, P])
        consts = sb("consts", [P, C_ALL])
        g_col = sb("g_col", [P, KT])
        o_scale = sb("o_scale", [P, 2])
        b_row = sb("b_row", [P, HEADS])
        lam_dot = sb("lam_dot", [P, 2])
        lam_exp = sb("lam_exp", [P, 2])
        neg_lam = sb("neg_lam", [P, 1])
        ssq = sb("ssq", [P, M_TILES])
        ms = sb("ms", [P, M_TILES])
        neg_half = sb("neg_half", [P, M_TILES])
        rstd = sb("rstd", [P, M_TILES])
        fl = sb("fl", [P, M_TILES, HEADS])
        fl_abs = sb("fl_abs", [P, M_TILES, HEADS])
        log_f = sb("log_f", [P, M_TILES, HEADS])
        c_nat = sb("c_nat", [P, M_TILES, HEADS])
        c_neg = sb("c_neg", [HEADS, SEQ])
        qkv_nat = sb("qkv_nat", [P, M_TILES, 3, HD])
        qkT_hi = sb("qkT_hi", [P, 2, SEQ], fp32r)
        qkT_lo = sb("qkT_lo", [P, 2, SEQ], fp32r)
        v_hi = sb("v_hi", [P, M_TILES, HD], fp32r)
        v_lo = sb("v_lo", [P, M_TILES, HD], fp32r)
        bias = sb("bias", [P, 3 * P])
        probs = sb("probs", [P, 2, 3 * P])
        wait_slot = sb("wait_slot", [P, 1])
        row_max = sb("row_max", [P, 4])
        neg_max = sb("neg_max", [P, 4])
        sums = sb("sums", [P, 4])
        inv = sb("inv", [P, 4])
        pT_hi = sb("pT_hi", [P, 3 * P], fp32r)
        pT_lo = sb("pT_lo", [P, 3 * P], fp32r)
        gate_tanh = sb("gate_tanh", [P, M_TILES, HD])
        gate = sb("gate", [P, M_TILES, HD])
        og = sb("og", [P, M_TILES, HD])
        o_ssq = sb("o_ssq", [P, M_TILES])
        o_ms = sb("o_ms", [P, M_TILES])
        o_rstd = sb("o_rstd", [P, M_TILES])
        y_ssq = sb("y_ssq", [P, M_TILES, 4])
        y_part = sb("y_part", [P, M_TILES])
        last_hi = oT_hi[:].rearrange("p (t a) n -> p t (a n)", t=4).rearrange("p t (k n) -> p t k n", k=2)
        last_lo = oT_lo[:].rearrange("p (t a) n -> p t (a n)", t=4).rearrange("p t (k n) -> p t k n", k=2)
        early = diff_z[:, 1, :]
        wfl = early[:, 0:P].rearrange("p (k h) -> p k h", k=KT)
        lam_in = early[:, P:P + 4 * QK].rearrange("p (i d) -> p i d", i=4)
        lam_tmp = early[:, 3 * P:4 * P].rearrange("p (i d) -> p i d", i=2)
        ones = early[:, 4 * P:5 * P]
        gn_rows = early[0:KT, 5 * P:6 * P]
        flT = early[0:2 * HEADS, 6 * P:6 * P + SEQ]
        wfl_parts = qkT_hi[:].rearrange("p i n -> p (i n)")[:, 0:KT * 2 * HEADS + P - 2 * HEADS]
        wfl_v = wfl_parts[:, 0:KT * 2 * HEADS].rearrange("p (k c) -> p k c", c=2 * HEADS)

        mask = consts[:, C_MASK:C_MASK + P]
        zero_mask = consts[:, C_ZERO:C_ZERO + 2 * P]
        tri = consts[:, C_TRI:C_TRI + P]
        cos = consts[:, C_COS:C_COS + 16].rearrange("p (m c) -> p m c", m=M_TILES)
        sin = consts[:, C_SIN:C_SIN + 16].rearrange("p (m c) -> p m c", m=M_TILES)
        sum_parts = consts[0:2 * HEADS, C_SEL:C_SEL + HEADS]
        x_sb = diff_z[:, 0, :].rearrange("p (m n) -> p m n", m=M_TILES)
        y_sb = diff_z[:, 1, :].rearrange("p (m n) -> p m n", m=M_TILES)
        m_a = diff_z[:, 1, 0:2 * CHUNK].rearrange("p (m n) -> p m n", m=M_TILES)
        m_b = diff_z[:, 1, 2 * CHUNK:4 * CHUNK].rearrange("p (m n) -> p m n", m=M_TILES)
        rope_t = fox_z[:, 0, 0:4 * 4 * HEADS * ROPE_HALF].rearrange("p (i b c) -> p i b c", i=4, c=ROPE_HALF)
        yg = fox_z[:, 0, :].rearrange("p (m n) -> p m n", m=M_TILES)
        square_out = fox_z[:, 1, :].rearrange("p (m n) -> p m n", m=M_TILES)

        Z = [bank(f"Z{i}") for i in range(4)]
        A, B, C, Dk = bank("A"), bank("B"), bank("C"), bank("Dk")
        T_BANKS = [A, B, C, Dk]

        SMALL = 16 * 7

        raw_loaded = [sem(f"raw_loaded{i}") for i in range(RING)]
        hi_ready, lo_ready, w_used = sem("hi_ready"), sem("lo_ready"), sem("w_used")
        evac = [sem("evac0"), sem("evac1")]
        x_loaded = [sem(f"x_loaded{i}") for i in range(TILES)]
        ident_ready, gn_loaded, small_loaded = sem("ident_ready"), sem("gn_loaded"), sem("small_loaded")
        wfl_loaded = sem("wfl_loaded")
        gT_done, g_col_ready = sem("gT_done"), sem("g_col_ready")
        xT_done, xh_ready, xl_ready = sem("xT_done"), sem("xh_ready"), sem("xl_ready")
        x_squared, ms_ready, rstd_ready = sem("x_squared"), sem("ms_ready"), sem("rstd_ready")
        pool_const = sem("pool_const")
        wfl_hi_ready, wfl_ready = sem("wfl_hi_ready"), sem("wfl_ready")
        flT_done, flT_ready = sem("flT_done"), sem("flT_ready")
        fl_done, fl_ready, softplus_ready, log_f_ready = sem("fl_done"), sem("fl_ready"), sem("softplus_ready"), sem("log_f_ready")
        c_done, c_nat_ready, cT_done, c_neg_ready = sem("c_done"), sem("c_nat_ready"), sem("cT_done"), sem("c_neg_ready")
        c_stored, rows_loaded = sem("c_stored"), sem("rows_loaded")
        lam_dots, lam_exps, lam_ready = sem("lam_dots"), sem("lam_exps"), sem("lam_ready")
        act_step, dve_step, pool_step = sem("act_step"), sem("dve_step"), sem("pool_step")
        scale_ready, tanh_ready = sem("scale_ready"), sem("tanh_ready")
        qkv_ready, bias_ready = sem("qkv_ready"), sem("bias_ready")
        v_hi_ready, v_ready = sem("v_hi_ready"), sem("v_ready")
        qkT_done, qkT_hi_ready, qkT_ready = sem("qkT_done"), sem("qkT_hi_ready"), sem("qkT_ready")
        scores_done, max_ready, exp_done, probs_ready = sem("scores_done"), sem("max_ready"), sem("exp_done"), sem("probs_ready")
        pT_done, pT_hi_ready, pT_ready, o_done = sem("pT_done"), sem("pT_hi_ready"), sem("pT_ready"), sem("o_done")
        o_ms_ready = sem("o_ms_ready")
        o_squared, o_rstd_ready, og_ready = sem("o_squared"), sem("o_rstd_ready"), sem("og_ready")
        oT_done, oT_hi_ready, oT_lo_ready = sem("oT_done"), sem("oT_hi_ready"), sem("oT_lo_ready")
        merge_tanh, m_ready, mT_done = sem("merge_tanh"), sem("m_ready"), sem("mT_done")
        mT_hi_ready, mT_lo_ready = sem("mT_hi_ready"), sem("mT_lo_ready")
        xres_loaded, gf_loaded = sem("xres_loaded"), sem("gf_loaded")
        y_squared, yg_ready = sem("y_squared"), sem("yg_ready")
        y_ms_ready, y_rstd_ready = sem("y_ms_ready"), sem("y_rstd_ready")
        out_ready, out_stored = [sem("out_ready0"), sem("out_ready1")], sem("out_stored")

        block = ctx.enter_context(nc.Block())

        @block.sync
        def _(sp):
            def load(c, j, src):
                if not (isinstance(c, int) and 8 * c + j < RING):
                    sp.wait_ge(lo_ready, 8 * c + (j - RING + 1))
                sp.dma_start(w_raw[:, j % RING], src).then_inc(raw_loaded[j % RING], 16)

            for j in range(TILES):
                sp.dma_start(x_sb[:, :, 2 * j * P:(2 * j + 2) * P], x_v[:, :, 2 * j * P:(2 * j + 2) * P]).then_inc(x_loaded[j], 16)
                load(0, j, w_in_v[:, 2 * j:2 * j + 2, FOX_COL:FOX_COL + CHUNK])
            with sp.Fori(1, 8) as c:
                for j in range(TILES):
                    load(c, j, w_in_v[:, 2 * j:2 * j + 2, ds(c * CHUNK + FOX_COL, CHUNK)])
            with sp.Fori(8, 16) as c:
                for j in range(TILES):
                    load(c, j, w_in_v[:, 2 * j:2 * j + 2, ds(c * CHUNK + (DIFF_COL - 8 * CHUNK), CHUNK)])
            with sp.Fori(16, 24) as c:
                for j in range(TILES):
                    load(c, j, w_in_v[:, 2 * j:2 * j + 2, ds(c * CHUNK + (MERGE_COL - 16 * CHUNK), CHUNK)])
            with sp.Fori(24, 28) as c:
                for j in range(TILES):
                    w = w_a_v if j < 4 else w_b_v
                    k = 2 * (j % 4)
                    load(c, j, w[:, k:k + 2, ds(c * CHUNK - 24 * CHUNK, CHUNK)])
            sp.wait_ge(oT_done, 2 * HEADS)
            sp.dma_start(x_sb, x_v).then_inc(xres_loaded, 16)
            sp.dma_start(rows[:], g_final.rearrange("(a n) -> a n", a=1).to_broadcast([P, D_MODEL])).then_inc(gf_loaded, 16)
            with sp.Fori(28, 32) as c:
                for j in range(TILES):
                    load(c, j, w_out_v[:, 2 * j:2 * j + 2, ds(c * CHUNK - 28 * CHUNK, CHUNK)])
            for m in range(M_TILES):
                sp.wait_ge(out_ready[1], m + 1)
                sp.dma_start(out_v[:, m, 2 * CHUNK:], yg[:, m, 2 * CHUNK:]).then_inc(out_stored, 16)
            sp.wait_ge(out_stored, 4 * 16)

        @block.tensor
        def _(pe):
            def split_product(acc, a_hi, a_lo, b_hi, b_lo, first, last):
                pe.matmul(acc, a_hi, b_hi, start=first, stop=False)
                pe.matmul(acc, a_hi, b_lo, start=False, stop=False)
                return pe.matmul(acc, a_lo, b_hi, start=False, stop=last)

            def tile(c, j, pair, stat_hi, stat_lo, k0, first, last):
                pe.wait_ge(hi_ready, 8 * c + (j + 1))
                pe.wait_ge(lo_ready, 8 * c + (j + 1))
                for kk in range(2):
                    for m in range(M_TILES):
                        tok = slice(m * P, (m + 1) * P)
                        mm = split_product(Z[2 * pair + m][:], stat_hi[:, k0 + kk, tok], stat_lo[:, k0 + kk, tok],
                                           w_hi[:, j % RING, kk], w_lo[:, j % RING, kk], first and kk == 0, last and kk == 1)
                mm.then_inc(w_used, 1)

            def banks_free(fill):
                pe.wait_ge(evac[0], fill - 1)
                pe.wait_ge(evac[1], fill - 1)

            def z_tile(c, j, pair):
                tile(c, j, pair, hT_hi, hT_lo, 2 * j, j == 0, j == TILES - 1)

            def x_transposes(j):
                pe.wait_ge(x_loaded[j], 16)
                if j == 3:
                    pe.wait_ge(g_col_ready, 1)
                if j >= 4:
                    pe.wait_ge(xl_ready, j - 3)
                for kk in range(2):
                    for m in range(M_TILES):
                        k = 2 * j + kk
                        mm = pe.transpose(T_BANKS[j % 4][:, (2 * kk + m) * P:(2 * kk + m + 1) * P],
                                          x_sb[:, m, k * P:(k + 1) * P], ident[:])
                mm.then_inc(xT_done, 1)

            def head_transposes(g):
                pe.wait_ge(qkv_ready, g + 1)
                for i in range(2):
                    for m in range(M_TILES):
                        mm = pe.transpose(A[:, (2 * i + m) * P:(2 * i + m + 1) * P], qkv_nat[:, m, i, :], ident[:])
                mm.then_inc(qkT_done, 1)

            def scores(g, maps):
                pe.wait_ge(qkT_ready, g + 1)
                for i in range(maps):
                    part = slice(0, P) if maps == 1 else slice(i * QK, (i + 1) * QK)
                    for q, keys, cols in ((slice(0, P), slice(0, P), slice(0, P)),
                                          (slice(P, 2 * P), slice(0, 2 * P), slice(P, 3 * P))):
                        mm = split_product((B, C)[i][:, cols], qkT_hi[part, 0, q], qkT_lo[part, 0, q],
                                           qkT_hi[part, 1, keys], qkT_lo[part, 1, keys], True, True)
                mm.then_inc(scores_done, 1)

            def prob_transposes(ready, count):
                pe.wait_ge(ready, count)
                for b in range(3):
                    mm = pe.transpose(Dk[:, b * P:(b + 1) * P], probs[:, 0, b * P:(b + 1) * P], ident[:])
                mm.then_inc(pT_done, 1)

            def values(g):
                pe.wait_ge(v_ready, g + 1)
                pe.wait_ge(pT_ready, g + 1)
                for b, (q, k) in enumerate(((0, 0), (1, 0), (1, 1))):
                    cols = slice(b * P, (b + 1) * P)
                    mm = split_product(A[:, q * P:(q + 1) * P], pT_hi[:, cols], pT_lo[:, cols],
                                       v_hi[:, k, :], v_lo[:, k, :], b < 2, b != 1)
                mm.then_inc(o_done, 1)

            def gated_transposes(g):
                pe.wait_ge(og_ready, g + 1)
                for m in range(M_TILES):
                    mm = pe.transpose(Dk[:, m * P:(m + 1) * P], og[:, m, :], ident[:])
                mm.then_inc(oT_done, 1)

            def merged_transposes(n):
                pe.wait_ge(m_ready, n + 1)
                for i in range(4):
                    for m in range(M_TILES):
                        mm = pe.transpose((A, B)[i // 2][:, (2 * (i % 2) + m) * P:(2 * (i % 2) + m + 1) * P],
                                          m_a[:, m, i * P:(i + 1) * P], ident[:])
                mm.then_inc(mT_done, 1)

            pe.wait_ge(ident_ready, 2)
            pe.wait_ge(gn_loaded, 16)
            pe.matmul(Dk[:, 0:KT], gn_rows, ident[0:KT, 0:KT], start=True, stop=True).then_inc(gT_done, 1)
            x_transposes(0)
            x_transposes(1)
            for j in range(TILES):
                pe.wait_ge(xh_ready, j + 1)
                pe.wait_ge(xl_ready, j + 1)
                z_tile(0, j, 0)
                if j + 2 < TILES:
                    x_transposes(j + 2)
            pe.wait_ge(wfl_ready, 3)
            for k in range(KT):
                for n, part in enumerate((hT_hi, hT_lo)):
                    mm = pe.matmul(A[:, 0:SEQ], wfl_parts[:, 2 * HEADS * k:2 * HEADS * k + P], part[:, k, :],
                                   start=(k == 0 and n == 0), stop=(k == KT - 1 and n == 1))
            mm.then_inc(flT_done, 1)
            for j in range(TILES):
                z_tile(1, j, 1)
                if j == 0:
                    pe.wait_ge(flT_ready, 1)
                    pe.wait_ge(small_loaded, SMALL)
                    for m in range(M_TILES):
                        mm = pe.matmul(B[:, m * HEADS:(m + 1) * HEADS], flT[:, m * P:(m + 1) * P], sum_parts, start=True, stop=True)
                    mm.then_inc(fl_done, 1)
                if j == 2:
                    pe.wait_ge(log_f_ready, 1)
                    pe.wait_ge(pool_const, 2)
                    pe.matmul(B[:, 0:HEADS], tri, log_f[:, 0, :], start=True, stop=True)
                    pe.matmul(B[:, HEADS:2 * HEADS], ones, log_f[:, 0, :], start=True, stop=False)
                    pe.matmul(B[:, HEADS:2 * HEADS], tri, log_f[:, 1, :], start=False, stop=True).then_inc(c_done, 1)
                if j == 4:
                    pe.wait_ge(c_nat_ready, 1)
                    for m in range(M_TILES):
                        mm = pe.matmul(C[0:HEADS, m * P:(m + 1) * P], c_nat[:, m, :], ident[:], start=True, stop=True)
                    mm.then_inc(cT_done, 1)

            with pe.Fori(1, 4) as i:
                for half in range(2):
                    c = 2 * i + half
                    banks_free(c)
                    for j in range(TILES):
                        z_tile(c, j, half)
            with pe.Fori(4, 8) as i:
                for half in range(2):
                    c = 2 * i + half
                    banks_free(c)
                    for j in range(TILES):
                        z_tile(c, j, half)
                        if j == 0:
                            head_transposes(c - 8)
                        if j == 1:
                            scores(c - 8, 1)
                        if j == 4:
                            prob_transposes(exp_done, c - 7)
                        if j == 5:
                            values(c - 8)
                        if j == 7:
                            gated_transposes(c - 8)
            with pe.Fori(8, 12) as i:
                for half in range(2):
                    c = 2 * i + half
                    banks_free(c)
                    for j in range(TILES):
                        z_tile(c, j, half)
                        if j == 0:
                            head_transposes(c - 8)
                        if j == 1:
                            scores(c - 8, 2)
                        if j == 4:
                            prob_transposes(probs_ready, c - 15)
                        if j == 5:
                            values(c - 8)
                        if j == 7:
                            gated_transposes(c - 8)

            def projection(n):
                for j in range(TILES):
                    if j % 4 == 0:
                        banks_free(2 * n + (24 + j // 4))
                    if j < 4 and isinstance(n, int):
                        pe.wait_ge(oT_lo_ready, HEADS + 2 * j + 2)
                    tile(n + 24, j, j // 4, oT_hi, oT_lo, (HEADS if j < 4 else 0) + 2 * (j % 4), j % 4 == 0, j % 4 == 3)
                    if j == 1 and not isinstance(n, int):
                        merged_transposes(n - 1)

            projection(0)
            with pe.Fori(1, 4) as n:
                projection(n)
            for n in range(3):
                c = 28 + n
                banks_free(32 + n)
                for j in range(TILES):
                    if n == 0:
                        pe.wait_ge(mT_lo_ready, j + 1)
                    z_tile(c, j, n % 2)
                    if n == 0 and j == 1:
                        merged_transposes(3)
            banks_free(35)
            for m in range(M_TILES):
                tok = slice(m * P, (m + 1) * P)
                for j in range(TILES):
                    if m == 0:
                        pe.wait_ge(hi_ready, 8 * 31 + j + 1)
                        pe.wait_ge(lo_ready, 8 * 31 + j + 1)
                    hi, lo = (last_hi[:, j], last_lo[:, j]) if j < 4 else (w_hi[:, j % RING], w_lo[:, j % RING])
                    for kk in range(2):
                        k = 2 * j + kk
                        mm = split_product(Z[2 + m][:], hT_hi[:, k, tok], hT_lo[:, k, tok], hi[:, kk], lo[:, kk],
                                           k == 0, k == KT - 1)
                mm.then_inc(w_used, 1)

        @block.scalar
        def _(act):
            def split(c, j):
                act.wait_ge(w_used, 8 * c + (j + 1))
                act.wait_ge(raw_loaded[j % RING], 32 * c + (16 * (2 + (j >= 4))))
                act.activation(w_hi[:, j % RING], w_raw[:, j % RING], ACT.Copy).then_inc(hi_ready, 1)

            def evacuate(c, half, z, col):
                act.wait_ge(w_used, 8 * c + 8)
                act.activation(z[:, 0, ds(col, CHUNK)], Z[2 * half][:], ACT.Copy, scale=rstd[:, 0:1]).then_inc(evac[0], 1)

            def x_part(j):
                act.wait_ge(xT_done, j + 1)
                for kk in range(2):
                    k = 2 * j + kk
                    ins = act.activation(hT_hi[:, k, :], T_BANKS[j % 4][:, kk * SEQ:(kk + 1) * SEQ], ACT.Copy,
                                         scale=g_col[:, k:k + 1])
                ins.then_inc(xh_ready, 1)

            act.dma_start(gn_rows, g_norm[0].rearrange("(k p) -> k p", p=P)).then_inc(gn_loaded, 16)
            act.wait_ge(g_col_ready, 1)
            for j in range(RING):
                x_part(j)
                act.wait_ge(raw_loaded[j], 16)
                act.activation(w_hi[:, j], w_raw[:, j], ACT.Copy).then_inc(hi_ready, 1)
            for j in range(TILES):
                if j < 4:
                    x_part(j + 4)
                if j in (4, 5):
                    m = j - 4
                    act.activation(square_out[:, m, :], x_sb[:, m, :], ACT.Square, accum_out=ssq[:, m:m + 1]).then_inc(x_squared, 1)
                if j == 6:
                    act.wait_ge(wfl_loaded, 16)
                    act.activation(wfl_v[:, :, 0:HEADS], wfl, ACT.Copy).then_inc(wfl_hi_ready, 1)
                split(0, j)
            act.wait_ge(rstd_ready, 1)
            evacuate(0, 0, fox_z, 0)
            for j in range(TILES):
                if j == 0:
                    act.wait_ge(fl_ready, 1)
                    act.activation(fl_abs[:], fl[:], ACT.Abs).then_inc(act_step, 1)
                    act.wait_ge(act_step, 1)
                    act.activation(fl_abs[:], fl_abs[:], ACT.Exp, scale=-1.0).then_inc(act_step, 1)
                    act.wait_ge(act_step, 2)
                    act.activation(fl_abs[:], fl_abs[:], ACT.Ln, bias=1.0).then_inc(softplus_ready, 1)
                if j == 6:
                    act.wait_ge(lam_dots, 2)
                    act.activation(lam_exp[:], lam_dot[:], ACT.Exp).then_inc(lam_exps, 1)
                split(1, j)
            evacuate(1, 1, fox_z, CHUNK)
            with act.Fori(1, 4) as i:
                for half in range(2):
                    c = 2 * i + half
                    for j in range(TILES):
                        split(c, j)
                    evacuate(c, half, fox_z, c * CHUNK)

            def qkT_hi_part(g, q_scale):
                act.wait_ge(qkT_done, g + 1)
                if q_scale is None:
                    act.activation(qkT_hi[:].rearrange("p i n -> p (i n)"), A[:], ACT.Copy).then_inc(qkT_hi_ready, 1)
                else:
                    act.activation(qkT_hi[:, 0, :], A[:, 0:SEQ], ACT.Copy, scale=q_scale)
                    act.activation(qkT_hi[:, 1, :], A[:, SEQ:2 * SEQ], ACT.Copy).then_inc(qkT_hi_ready, 1)

            def pT_hi_part(g):
                act.wait_ge(pT_done, g + 1)
                act.activation(pT_hi[:], Dk[:, 0:3 * P], ACT.Copy).then_inc(pT_hi_ready, 1)

            def tanh(z, h, n):
                act.wait_ge(evac[0], n)
                act.wait_ge(evac[1], n)
                act.activation(gate_tanh[:], z[:, :, ds(h * HD + G_OFF, HD)], ACT.Tanh, scale=0.5).then_inc(tanh_ready, 1)

            def exps(g, maps, scale):
                act.wait_ge(max_ready, g + 1)
                for i in range(maps):
                    act.activation(probs[:, i, 0:P], probs[:, i, 0:P], ACT.Exp, bias=neg_max[:, 2 * i:2 * i + 1],
                                   scale=scale, accum_out=sums[:, 2 * i:2 * i + 1])
                    ins = act.activation(probs[:, i, P:3 * P], probs[:, i, P:3 * P], ACT.Exp,
                                         bias=neg_max[:, 2 * i + 1:2 * i + 2], scale=scale,
                                         accum_out=sums[:, 2 * i + 1:2 * i + 2])
                ins.then_inc(exp_done, 1)

            def gated_hi(g, branch):
                act.wait_ge(oT_done, g + 1)
                act.activation(oT_hi[:, ds(g, 1), :], Dk[:, 0:SEQ].rearrange("p (a n) -> p a n", a=1), ACT.Copy,
                               scale=o_scale[:, branch:branch + 1]).then_inc(oT_hi_ready, 1)

            act.wait_ge(scale_ready, 2)
            with act.Fori(4, 8) as i:
                for half in range(2):
                    c = 2 * i + half
                    for j in range(TILES):
                        if j == 0:
                            qkT_hi_part(c - 8, HD ** -0.5)
                        if j == 4:
                            pT_hi_part(c - 8)
                        if j == 7:
                            gated_hi(c - 8, 0)
                        split(c, j)
                        if j == 1:
                            exps(c - 8, 1, 1.0)
                        if j == 2:
                            tanh(fox_z, c - 8, 8)
                    evacuate(c, half, diff_z, c * CHUNK - 8 * CHUNK)
            with act.Fori(8, 12) as i:
                for half in range(2):
                    c = 2 * i + half
                    for j in range(TILES):
                        if j == 0:
                            qkT_hi_part(c - 8, None)
                        if j == 4:
                            pT_hi_part(c - 8)
                        if j == 5:
                            act.wait_ge(o_done, c - 7)
                            for m in range(M_TILES):
                                ins = act.activation(gate_tanh[:, m, :], A[:, m * P:(m + 1) * P], ACT.Square,
                                                     accum_out=o_ssq[:, m:m + 1])
                            ins.then_inc(o_squared, 1)
                        if j == 7:
                            gated_hi(c - 8, 1)
                        split(c, j)
                        if j == 1:
                            exps(c - 8, 2, QK ** -0.5)
                        if j == 2:
                            tanh(diff_z, c - 16, 16)
                    evacuate(c, half, fox_z, c * CHUNK - 16 * CHUNK)

            def merged_hi(n):
                act.wait_ge(mT_done, n + 1)
                for b in range(2):
                    act.activation(hT_hi[:, ds(4 * n + 2 * b, 2), :], (A, B)[b][:].rearrange("p (a n) -> p a n", a=2),
                                   ACT.Copy, scale=0.5).then_inc(mT_hi_ready, 1)

            def projection(n):
                for j in range(TILES):
                    if j < 2:
                        z = fox_z[:, :, ds(n * CHUNK + j * D_MODEL, CHUNK)]
                        act.activation(z, z, ACT.Tanh, scale=0.5).then_inc(merge_tanh, 1)
                    if j == 2 and not isinstance(n, int):
                        merged_hi(n - 1)
                    split(n + 24, j)

            act.wait_ge(evac[1], 24)
            act.wait_ge(evac[0], 24)
            projection(0)
            with act.Fori(1, 4) as n:
                projection(n)
            def square(m, n):
                act.wait_ge(evac[m], 33 + n)
                act.activation(fox_z[:, 1, m * D_MODEL + n * CHUNK:m * D_MODEL + (n + 1) * CHUNK], y_sb[:, m, n * CHUNK:(n + 1) * CHUNK],
                               ACT.Square, accum_out=y_ssq[:, m, n:n + 1]).then_inc(y_squared, 1)

            for n in range(3):
                for j in range(TILES):
                    if n == 0 and j == 2:
                        merged_hi(3)
                    if n == 2 and j >= 4:
                        act.wait_ge(raw_loaded[j % RING], 16 * 63)
                        act.activation(last_hi[:, j - 4], w_raw[:, j % RING], ACT.Copy).then_inc(hi_ready, 1)
                    else:
                        split(28 + n, j)
                for m in range(M_TILES):
                    square(m, n)
            for j in range(4, TILES):
                act.wait_ge(w_used, 8 * 30 + j + 1)
                act.wait_ge(raw_loaded[j % RING], 16 * 64)
                act.activation(w_hi[:, j % RING], w_raw[:, j % RING], ACT.Copy).then_inc(hi_ready, 1)
            for m in range(M_TILES):
                square(m, 3)
                act.wait_ge(yg_ready, 6)
                act.wait_ge(y_rstd_ready, m + 1)
                act.activation(yg[:, m, 0:2 * CHUNK], yg[:, m, 0:2 * CHUNK], ACT.Copy, scale=rstd[:, m:m + 1]).then_inc(out_ready[0], 1)
                act.wait_ge(out_ready[0], m + 1)
                act.dma_start(out_v[:, m, 0:2 * CHUNK], yg[:, m, 0:2 * CHUNK]).then_inc(out_stored, 16)

        @block.vector
        def _(dve):
            step = [0]

            def chained(ins):
                step[0] += 1
                ins.then_inc(dve_step, 1)
                dve.wait_ge(dve_step, step[0])

            def split(c, j):
                dve.wait_ge(hi_ready, 8 * c + (j + 5))
                dve.tensor_tensor(w_lo[:, j % RING], w_raw[:, j % RING], w_hi[:, j % RING].bitcast(fp32),
                                  ALU.subtract).then_inc(lo_ready, 1)

            def evacuate(c, half, z, col):
                dve.wait_ge(w_used, 8 * c + 8)
                dve.tensor_scalar(z[:, 1, ds(col, CHUNK)], Z[2 * half + 1][:], rstd[:, 1:2], None,
                                  ALU.mult).then_inc(evac[1], 1)

            def x_part(j):
                dve.wait_ge(xh_ready, j + 1)
                for kk in range(2):
                    k = 2 * j + kk
                    ins = dve.scalar_tensor_tensor(hT_lo[:, k, :], T_BANKS[j % 4][:, kk * SEQ:(kk + 1) * SEQ],
                                                   g_col[:, k:k + 1], hT_hi[:, k, :].bitcast(fp32), ALU.mult, ALU.subtract)
                ins.then_inc(xl_ready, 1)

            dve.memset(wfl_parts[:, KT * 2 * HEADS:].bitcast(fp32), 0.0).then_inc(wfl_ready, 1)
            dve.memset(o_scale[:, 0:1], 0.5).then_inc(scale_ready, 1)
            dve.wait_ge(gT_done, 1)
            dve.tensor_copy(g_col[:], Dk[:, 0:KT]).then_inc(g_col_ready, 1)
            for j in range(RING):
                x_part(j)
                dve.wait_ge(hi_ready, j + 1)
                dve.tensor_tensor(w_lo[:, j], w_raw[:, j], w_hi[:, j].bitcast(fp32), ALU.subtract).then_inc(lo_ready, 1)
            for j in range(TILES):
                if j < 4:
                    x_part(j + 4)
                if j == 6:
                    dve.wait_ge(x_squared, 2)
                    dve.tensor_scalar(ms[:], ssq[:], 1.0 / D_MODEL, EPS, ALU.mult, ALU.add).then_inc(ms_ready, 1)
                if j == 7:
                    dve.wait_ge(wfl_hi_ready, 1)
                    dve.tensor_tensor(wfl_v[:, :, HEADS:2 * HEADS], wfl, wfl_v[:, :, 0:HEADS].bitcast(fp32),
                                      ALU.subtract).then_inc(wfl_ready, 2)
                split(0, j)
            dve.wait_ge(rstd_ready, 1)
            evacuate(0, 0, fox_z, 0)
            for j in range(TILES):
                if j == 0:
                    dve.wait_ge(flT_done, 1)
                    dve.tensor_copy(flT, A[0:2 * HEADS, 0:SEQ]).then_inc(flT_ready, 1)
                    dve.wait_ge(fl_done, 1)
                    dve.wait_ge(small_loaded, SMALL)
                    for m in range(M_TILES):
                        ins = dve.scalar_tensor_tensor(fl[:, m, :], B[:, m * HEADS:(m + 1) * HEADS], rstd[:, m:m + 1], b_row[:],
                                                       ALU.mult, ALU.add)
                    ins.then_inc(fl_ready, 1)
                if j == 1:
                    dve.wait_ge(softplus_ready, 1)
                    dve.scalar_tensor_tensor(log_f[:], fl[:], 0.0, fl_abs[:], ALU.min, ALU.subtract).then_inc(log_f_ready, 1)
                if j == 2:
                    dve.wait_ge(c_done, 1)
                    dve.tensor_copy(c_nat[:].rearrange("p m h -> p (m h)"), B[:, 0:2 * HEADS]).then_inc(c_nat_ready, 1)
                if j == 4:
                    dve.wait_ge(cT_done, 1)
                    dve.tensor_scalar(c_neg[:], C[0:HEADS, 0:SEQ], -1.0, None, ALU.mult).then_inc(c_neg_ready, 1)
                if j == 5:
                    for i in range(2):
                        dve.tensor_tensor_reduce(lam_tmp[:, i], lam_in[:, 2 * i, :], lam_in[:, 2 * i + 1, :], 1.0, 0.0,
                                                 ALU.mult, ALU.add, lam_dot[:, i:i + 1]).then_inc(lam_dots, 1)
                if j == 7:
                    dve.wait_ge(lam_exps, 1)
                    chained(dve.tensor_tensor(neg_lam[:], lam_exp[:, 1:2], lam_exp[:, 0:1], ALU.subtract))
                    dve.tensor_scalar(neg_lam[:], neg_lam[:], -LAM_INIT, None, ALU.add).then_inc(lam_ready, 1)
                    dve.tensor_scalar(o_scale[:, 1:2], o_scale[:, 1:2], 0.5 * (1.0 - LAM_INIT), None, ALU.mult).then_inc(scale_ready, 1)
                split(1, j)
            evacuate(1, 1, fox_z, CHUNK)
            with dve.Fori(1, 4) as i:
                for half in range(2):
                    c = 2 * i + half
                    for j in range(TILES):
                        split(c, j)
                    evacuate(c, half, fox_z, c * CHUNK)

            def masked_max(S, i, add0, add1):
                if i == 0:
                    dve.memset(wait_slot[:], 0.0)
                dve.tensor_tensor_reduce(probs[:, i, 0:P], S[:, 0:P], add0, 1.0, NEG, ALU.add, ALU.max,
                                         row_max[:, 2 * i:2 * i + 1]).then_inc(dve_step, 1)
                dve.tensor_tensor_reduce(probs[:, i, P:3 * P], S[:, P:3 * P], add1, 1.0, NEG, ALU.add, ALU.max,
                                         row_max[:, 2 * i + 1:2 * i + 2]).then_inc(dve_step, 1)

            def qkT_lo_part(g, q_scale):
                dve.wait_ge(qkT_hi_ready, g + 1)
                if q_scale is None:
                    dve.tensor_tensor(qkT_lo[:].rearrange("p i n -> p (i n)"), A[:],
                                      qkT_hi[:].rearrange("p i n -> p (i n)").bitcast(fp32), ALU.subtract).then_inc(qkT_ready, 1)
                else:
                    dve.scalar_tensor_tensor(qkT_lo[:, 0, :], A[:, 0:SEQ], q_scale, qkT_hi[:, 0, :].bitcast(fp32),
                                             ALU.mult, ALU.subtract)
                    dve.tensor_tensor(qkT_lo[:, 1, :], A[:, SEQ:2 * SEQ], qkT_hi[:, 1, :].bitcast(fp32),
                                      ALU.subtract).then_inc(qkT_ready, 1)

            def pT_lo_part(g):
                dve.wait_ge(pT_hi_ready, g + 1)
                dve.tensor_tensor(pT_lo[:], Dk[:, 0:3 * P], pT_hi[:].bitcast(fp32), ALU.subtract).then_inc(pT_ready, 1)

            def gate_product(z, h, g):
                dve.wait_ge(tanh_ready, g + 1)
                dve.scalar_tensor_tensor(gate[:], gate_tanh[:], 1.0, z[:, :, ds(h * HD + G_OFF, HD)],
                                         ALU.add, ALU.mult).then_inc(dve_step, 1)

            def gated_lo(g, branch):
                dve.wait_ge(oT_hi_ready, g + 1)
                dve.scalar_tensor_tensor(oT_lo[:, ds(g, 1), :], Dk[:, 0:SEQ].rearrange("p (a n) -> p a n", a=1),
                                         o_scale[:, branch:branch + 1], oT_hi[:, ds(g, 1), :].bitcast(fp32),
                                         ALU.mult, ALU.subtract).then_inc(oT_lo_ready, 1)

            s0 = step[0]
            with dve.Fori(4, 8) as i:
                for half in range(2):
                    c = 2 * i + half
                    steps = 3 * c + (s0 - 24)
                    for j in range(TILES):
                        if j == 0:
                            qkT_lo_part(c - 8, HD ** -0.5)
                        if j == 1:
                            dve.wait_ge(scores_done, c - 7)
                            dve.wait_ge(bias_ready, 2 * c - 14)
                            masked_max(B, 0, bias[:, 0:P], bias[:, P:3 * P])
                            dve.wait_ge(dve_step, steps + 2)
                            dve.tensor_scalar(neg_max[:, 0:2], row_max[:, 0:2], -1.0, None, ALU.mult).then_inc(max_ready, 1)
                        if j == 3:
                            dve.wait_ge(exp_done, c - 7)
                            dve.reciprocal(inv[:, 0:2], sums[:, 0:2])
                            gate_product(fox_z, c - 8, c - 8)
                        if j == 4:
                            pT_lo_part(c - 8)
                        if j == 5:
                            dve.wait_ge(o_done, c - 7)
                            dve.wait_ge(dve_step, steps + 3)
                            for m in range(M_TILES):
                                ins = dve.scalar_tensor_tensor(og[:, m, :], A[:, m * P:(m + 1) * P], inv[:, m:m + 1],
                                                               gate[:, m, :], ALU.mult, ALU.mult)
                            ins.then_inc(og_ready, 1)
                        if j == 7:
                            gated_lo(c - 8, 0)
                        split(c, j)
                    evacuate(c, half, diff_z, c * CHUNK - 8 * CHUNK)
            s1 = s0 + 3 * HEADS
            with dve.Fori(8, 12) as i:
                for half in range(2):
                    c = 2 * i + half
                    steps = 9 * c + (s1 - 144)
                    for j in range(TILES):
                        if j == 0:
                            qkT_lo_part(c - 8, None)
                        if j == 1:
                            dve.wait_ge(scores_done, c - 7)
                            for mp, S in enumerate((B, C)):
                                masked_max(S, mp, mask, zero_mask)
                            dve.wait_ge(dve_step, steps + 4)
                            dve.tensor_scalar(neg_max[:], row_max[:], -(QK ** -0.5), None, ALU.mult).then_inc(max_ready, 1)
                        if j == 2:
                            dve.wait_ge(exp_done, c - 7)
                            dve.reciprocal(inv[:], sums[:]).then_inc(dve_step, 1)
                            dve.wait_ge(dve_step, steps + 5)
                            dve.tensor_scalar(inv[:, 2:4], inv[:, 2:4], neg_lam[:, 0:1], None, ALU.mult).then_inc(dve_step, 1)
                            dve.wait_ge(dve_step, steps + 6)
                            for m, sl in enumerate((slice(0, P), slice(P, 3 * P))):
                                dve.tensor_scalar(probs[:, 1, sl], probs[:, 1, sl], inv[:, 2 + m:3 + m], None,
                                                  ALU.mult).then_inc(dve_step, 1)
                            dve.wait_ge(dve_step, steps + 8)
                            for m, sl in enumerate((slice(0, P), slice(P, 3 * P))):
                                ins = dve.scalar_tensor_tensor(probs[:, 0, sl], probs[:, 0, sl], inv[:, m:m + 1],
                                                               probs[:, 1, sl], ALU.mult, ALU.add)
                            ins.then_inc(probs_ready, 1)
                        if j == 3:
                            gate_product(diff_z, c - 16, c - 8)
                        if j == 4:
                            pT_lo_part(c - 8)
                        if j == 5:
                            dve.wait_ge(o_squared, c - 15)
                            dve.tensor_scalar(o_ms[:], o_ssq[:], 1.0 / HD, EPS, ALU.mult, ALU.add).then_inc(o_ms_ready, 1)
                        if j == 6:
                            dve.wait_ge(o_rstd_ready, c - 15)
                            dve.wait_ge(dve_step, steps + 9)
                            for m in range(M_TILES):
                                ins = dve.scalar_tensor_tensor(og[:, m, :], A[:, m * P:(m + 1) * P], o_rstd[:, m:m + 1],
                                                               gate[:, m, :], ALU.mult, ALU.mult)
                            ins.then_inc(og_ready, 1)
                        if j == 7:
                            gated_lo(c - 8, 1)
                        split(c, j)
                    evacuate(c, half, fox_z, c * CHUNK - 16 * CHUNK)

            def merged_lo(n):
                for b in range(2):
                    dve.wait_ge(mT_hi_ready, 2 * n + (b + 1))
                    dve.scalar_tensor_tensor(hT_lo[:, ds(4 * n + 2 * b, 2), :], (A, B)[b][:].rearrange("p (a n) -> p a n", a=2),
                                             0.5, hT_hi[:, ds(4 * n + 2 * b, 2), :].bitcast(fp32),
                                             ALU.mult, ALU.subtract).then_inc(mT_lo_ready, 1)

            def gate_branch(n, branch, dst):
                dve.wait_ge(w_used, 8 * n + (8 * 24 + 4 + 4 * branch))
                dve.wait_ge(merge_tanh, 2 * n + (1 + branch))
                for m in range(M_TILES):
                    dve.scalar_tensor_tensor(dst[:, m, :], fox_z[:, m, ds(n * CHUNK + branch * D_MODEL, CHUNK)], 1.0,
                                             Z[2 * branch + m][:], ALU.add, ALU.mult).then_inc(evac[m], 1)

            def projection(n):
                for j in range(TILES):
                    if j == 2 and not isinstance(n, int):
                        merged_lo(n - 1)
                    split(n + 24, j)
                    if j == 3:
                        gate_branch(n, 0, m_a)
                gate_branch(n, 1, m_b)
                dve.wait_ge(evac[1], 2 * n + 26)
                dve.tensor_tensor(m_a, m_a, m_b, ALU.add).then_inc(m_ready, 1)

            projection(0)
            with dve.Fori(1, 4) as n:
                projection(n)
            dve.wait_ge(xres_loaded, 16)

            def residual(m, n):
                sl = slice(n * CHUNK, (n + 1) * CHUNK)
                dve.tensor_tensor(y_sb[:, m, sl], Z[2 * (n % 2) + m][:], x_sb[:, m, sl], ALU.add).then_inc(evac[m], 1)

            for n in range(3):
                for j in range(TILES):
                    if n == 0 and j == 2:
                        merged_lo(3)
                    if n == 2 and j >= 4:
                        dve.wait_ge(hi_ready, 8 * 31 + j - 3)
                        dve.tensor_tensor(last_lo[:, j - 4], w_raw[:, j % RING], last_hi[:, j - 4].bitcast(fp32),
                                          ALU.subtract).then_inc(lo_ready, 1)
                    else:
                        split(28 + n, j)
                dve.wait_ge(w_used, 8 * (29 + n))
                for m in range(M_TILES):
                    residual(m, n)
            for j in range(4):
                split(31, j)
            dve.wait_ge(y_squared, 6)
            dve.tensor_reduce(ssq[:], y_ssq[:, :, 0:3], AX.X, ALU.add).then_inc(y_ms_ready, 1)
            dve.wait_ge(y_ms_ready, 1)
            dve.tensor_scalar(y_part[:], ssq[:], 1.0 / D_MODEL, EPS, ALU.mult, ALU.add).then_inc(y_ms_ready, 1)
            dve.wait_ge(gf_loaded, 16)
            for m in range(M_TILES):
                dve.wait_ge(w_used, 8 * 31 + m + 1)
                residual(m, 3)
                dve.wait_ge(y_squared, 7 + m)
                dve.wait_ge(y_ms_ready, 2 + m)
                dve.tensor_scalar(ms[:, m:m + 1], y_ssq[:, m, 3:4], 1.0 / D_MODEL, y_part[:, m:m + 1],
                                  ALU.mult, ALU.add).then_inc(y_ms_ready, 1)
                dve.wait_ge(y_rstd_ready, m + 1)
                dve.wait_ge(yg_ready, 6)
                dve.tensor_scalar(yg[:, m, 2 * CHUNK:3 * CHUNK], yg[:, m, 2 * CHUNK:3 * CHUNK], rstd[:, m:m + 1], None, ALU.mult)
                dve.scalar_tensor_tensor(yg[:, m, 3 * CHUNK:], y_sb[:, m, 3 * CHUNK:], rstd[:, m:m + 1], rows[:, 3 * CHUNK:],
                                         ALU.mult, ALU.mult).then_inc(out_ready[1], 1)

        @block.gpsimd
        def _(pool):
            step = [0]

            def chained(ins):
                step[0] += 1
                ins.then_inc(pool_step, 1)
                pool.wait_ge(pool_step, step[0])

            pool.memset(ident[:], 0.0).then_inc(ident_ready, 1)
            pool.wait_ge(ident_ready, 1)
            pool.affine_select(out=ident[:], in_=ident[:], compare_op=ALU.not_equal, fill=1.0, base=0,
                               pattern=[[-1, P]], channel_multiplier=1).then_inc(ident_ready, 1)
            pool.dma_start(consts[:], consts_in).then_inc(small_loaded, 16)
            pool.dma_start(o_scale[:, 1:2], g_subln.rearrange("a d -> d a")).then_inc(small_loaded, 16)
            pool.dma_start(b_row[:], b_forget.to_broadcast([P, HEADS])).then_inc(small_loaded, 16)
            pool.dma_start(wfl, w_in_v[:, :, FL_COL:FL_COL + HEADS]).then_inc(wfl_loaded, 16)
            for i, v in enumerate((lq1, lk1, lq2, lk2)):
                pool.dma_start(lam_in[:, i, :], v.to_broadcast([P, QK])).then_inc(small_loaded, 16)
            pool.memset(ones, 1.0).then_inc(pool_const, 1)
            pool.memset(neg_half[:], -0.5).then_inc(pool_const, 1)
            pool.wait_ge(pool_const, 2)
            pool.wait_ge(ms_ready, 1)
            pool.tensor_tensor(rstd[:], ms[:], neg_half[:], ALU.pow).then_inc(rstd_ready, 1)
            pool.wait_ge(c_neg_ready, 1)
            pool.dma_start(c_rows_dram, c_neg[:]).then_inc(c_stored, 16)
            pool.wait_ge(c_stored, 16)
            pool.dma_start(rows[:], c_rows_dram.rearrange("(a h) n -> a (h n)", a=1).to_broadcast([P, HEADS * SEQ])).then_inc(rows_loaded, 16)

            def past(c):
                pool.wait_ge(w_used, 8 * c - 2)

            def head_copy(z, h, g=None):
                if g is not None:
                    pool.wait_ge(v_ready, g)
                src = z[:, :, 0:3 * WIDTH].rearrange("p m (i n) -> p m i n", i=3)[:, :, :, ds(h * HD, HD)]
                pool.tensor_copy(qkv_nat[:], src).then_inc(qkv_ready, 1)

            def head_v(z, h, g, c=None):
                if c is not None:
                    pool.wait_ge(w_used, 8 * c - 1)
                pool.tensor_copy(v_hi[:], z[:, :, ds(h * HD + V_OFF, HD)]).then_inc(v_hi_ready, 1)
                pool.wait_ge(qkv_ready, g + 1)
                pool.wait_ge(v_hi_ready, g + 1)
                pool.tensor_tensor(v_lo[:], qkv_nat[:, :, 2, :], v_hi[:].bitcast(fp32), ALU.subtract).then_inc(v_ready, 1)

            def head_bias(h, steps):
                for m, sl in enumerate((slice(0, P), slice(P, 3 * P))):
                    n = (m + 1) * P
                    pool.tensor_tensor(bias[:, sl], rows[:].rearrange("p (h n) -> p h n", h=HEADS)[:, ds(h, 1), 0:n],
                                       c_nat[:, m, ds(h, 1)].unsqueeze(2).to_broadcast([P, 1, n]),
                                       ALU.add).then_inc(pool_step, 1)
                pool.wait_ge(pool_step, steps)
                for sl in (slice(0, P), slice(2 * P, 3 * P)):
                    pool.tensor_tensor(bias[:, sl], bias[:, sl], mask, ALU.add).then_inc(bias_ready, 1)

            def evacuated(n):
                pool.wait_ge(evac[0], n)
                pool.wait_ge(evac[1], n)

            evacuated(6)
            pool.wait_ge(rows_loaded, 16)
            pool.wait_ge(c_nat_ready, 1)
            head_copy(fox_z, 0)
            head_bias(0, step[0] + 2)
            head_v(fox_z, 0, 0)
            with pool.Fori(9, 16) as c:
                past(c)
                head_copy(fox_z, c - 8, c - 8)
                head_bias(c - 8, 2 * c + (step[0] + 2 - 16))
                head_v(fox_z, c - 8, c - 8, c)
            step[0] += 2 * HEADS

            evacuated(12)
            for m in range(M_TILES):
                blocks = diff_z[:, m, 0:2 * WIDTH].rearrange("p (b d) -> p b d", d=QK)
                x1, x2 = blocks[:, :, 0:ROPE_HALF], blocks[:, :, ROPE_HALF:2 * ROPE_HALF]
                shape = [P, 2 * 2 * HEADS, ROPE_HALF]
                cos_m, sin_m = (t[:, m, :].unsqueeze(1).to_broadcast(shape) for t in (cos, sin))
                for i, (u, v) in enumerate(((x1, cos_m), (x2, sin_m), (x2, cos_m), (x1, sin_m))):
                    ins = pool.tensor_tensor(rope_t[:, i], u, v, ALU.mult)
                chained(ins)
                pool.tensor_tensor(x1, rope_t[:, 0], rope_t[:, 1], ALU.subtract)
                chained(pool.tensor_tensor(x2, rope_t[:, 2], rope_t[:, 3], ALU.add))
            evacuated(14)
            past(16)
            head_copy(diff_z, 0, 8)
            head_v(diff_z, 0, 8, 16)

            def head_rstd(c):
                pool.wait_ge(o_ms_ready, c - 15)
                pool.tensor_tensor(o_rstd[:], o_ms[:], neg_half[:], ALU.pow).then_inc(o_rstd_ready, 1)

            with pool.Fori(16, 23) as c:
                head_rstd(c)
                past(c + 1)
                head_copy(diff_z, c - 15, c - 7)
                head_v(diff_z, c - 15, c - 7, c + 1)
            head_rstd(23)

            pool.wait_ge(gf_loaded, 16)
            for n in range(3):
                sl = slice(n * CHUNK, (n + 1) * CHUNK)
                for m in range(M_TILES):
                    pool.wait_ge(evac[m], 33 + n)
                    pool.tensor_tensor(yg[:, m, sl], y_sb[:, m, sl], rows[:, sl], ALU.mult).then_inc(yg_ready, 1)
            for m in range(M_TILES):
                pool.wait_ge(y_ms_ready, 3 + m)
                pool.tensor_tensor(rstd[:, m:m + 1], ms[:, m:m + 1], neg_half[:, m:m + 1], ALU.pow).then_inc(y_rstd_ready, 1)


def kernel(x, g_norm, w_in, lambda_q1, lambda_k1, lambda_q2, lambda_k2, g_subln, b_forget,
           w_proj_a, w_proj_b, w_out, g_final):
    import concourse.bacc as bacc
    from concourse.bass_utils import run_bass_kernel_spmd

    pos = np.arange(SEQ, dtype=np.float32)
    inv_freq = np.float32(500000.0) ** (-np.arange(ROPE_HALF, dtype=np.float32) * 2.0 / (2 * ROPE_HALF))
    angle = (pos[:, None] * inv_freq[None, :].astype(np.float32)).reshape(M_TILES, P, ROPE_HALF).transpose(1, 0, 2)
    i = np.arange(P)
    consts = np.zeros((P, C_ALL), np.float32)
    consts[:, C_MASK:C_MASK + P] = np.where(i[:, None] >= i[None, :], 0.0, NEG)
    consts[:, C_TRI:C_TRI + P] = i[:, None] <= i[None, :]
    consts[0:2 * HEADS, C_SEL:C_SEL + HEADS] = np.tile(np.eye(HEADS), (2, 1))
    consts[:, C_COS:C_COS + 16] = np.cos(angle).reshape(P, 16)
    consts[:, C_SIN:C_SIN + 16] = np.sin(angle).reshape(P, 16)

    named = dict(x=x, g_norm=g_norm, w_in=w_in, lq1=lambda_q1, lk1=lambda_k1, lq2=lambda_q2, lk2=lambda_k2,
                 g_subln=g_subln, b_forget=b_forget, w_a=w_proj_a, w_b=w_proj_b, w_out=w_out, g_final=g_final,
                 consts=consts)
    nc = bacc.Bacc("TRN2", target_bir_lowering=False, num_devices=1)
    arrays, args = {}, []
    for name, value in named.items():
        a = np.ascontiguousarray(value)
        arrays[f"in_{name}"] = a
        args.append(nc.dram_tensor(f"in_{name}", a.shape, mybir.dt.from_np(a.dtype), kind="ExternalInput").ap())
    args.append(nc.dram_tensor("out_y", (1, SEQ, D_MODEL), mybir.dt.float32, kind="ExternalOutput").ap())
    build(nc, *args)
    r = run_bass_kernel_spmd(nc, [arrays], core_ids=[0])
    return r.results[0]["out_y"]
```

```python
import math

import numpy as np

import concourse.bass as bass
from concourse import mybir
from contextlib import ExitStack

P = 128
D_MODEL = 2048
SEQ = 256
M_TILES = SEQ // P
KT = D_MODEL // P
HEADS = 8
HD = 128
QK = 64
WIDTH = 1024
ROPE_HALF = 8
EPS = 1e-6
NEG = -3.0e38
LAM_INIT = 0.8 - 0.6 * math.exp(-0.3 * 0)
CHUNK = 512
RING = 4
TILES = 8
DIFF_COL = 0
FOX_COL = 4 * WIDTH
FL_COL = 8 * WIDTH
MERGE_COL = FL_COL + HEADS
G_OFF = 3 * WIDTH
C_ZERO, C_MASK, C_TRI, C_COS, C_SIN, C_SEL, C_ALL = 0, P, 2 * P, 3 * P, 3 * P + 16, 3 * P + 32, 3 * P + 40


def build(nc, x, g_norm, w_in, lq1, lk1, lq2, lk2, g_subln, b_forget, w_a, w_b, w_out, g_final,
          consts_in, out):
    fp32 = mybir.dt.float32
    fp32r = mybir.dt.float32r
    ALU = mybir.AluOpType
    ACT = mybir.ActivationFunctionType
    AX = mybir.AxisListType
    ds = bass.ds

    w_in_v = w_in[0].rearrange("(k p) n -> p k n", p=P)
    w_a_v = w_a[0].rearrange("(k p) n -> p k n", p=P)
    w_b_v = w_b[0].rearrange("(k p) n -> p k n", p=P)
    w_out_v = w_out[0].rearrange("(k p) n -> p k n", p=P)
    x_v = x[0].rearrange("(m p) n -> p m n", p=P)
    out_v = out[0].rearrange("(m p) n -> p m n", p=P)
    c_rows_dram = nc.dram_tensor("c_rows_dram", [HEADS, SEQ], fp32, kind="Internal").ap()

    ctx = ExitStack()
    with ctx:
        def sb(name, shape, dt=fp32):
            return ctx.enter_context(nc.sbuf_tensor(name, shape, dt))

        def bank(name):
            return ctx.enter_context(nc.psum_tensor(name, [P, 512], fp32))

        def sem(name):
            return ctx.enter_context(nc.semaphore(name))

        w_raw = sb("w_raw", [P, RING, 2, CHUNK])
        w_hi = sb("w_hi", [P, RING, 2, CHUNK], fp32r)
        w_lo = sb("w_lo", [P, RING, 2, CHUNK], fp32r)
        hT_hi = sb("hT_hi", [P, KT, SEQ], fp32r)
        hT_lo = sb("hT_lo", [P, KT, SEQ], fp32r)
        fox_z = sb("fox_z", [P, M_TILES, 4 * WIDTH])
        diff_z = sb("diff_z", [P, M_TILES, 4 * WIDTH])
        oT_hi = sb("oT_hi", [P, 2 * HEADS, SEQ], fp32r)
        oT_lo = sb("oT_lo", [P, 2 * HEADS, SEQ], fp32r)
        rows = sb("rows", [P, HEADS * SEQ])
        ident = sb("ident", [P, P])
        consts = sb("consts", [P, C_ALL])
        g_col = sb("g_col", [P, KT])
        o_scale = sb("o_scale", [P, 2])
        b_row = sb("b_row", [P, HEADS])
        lam_dot = sb("lam_dot", [P, 2])
        lam_exp = sb("lam_exp", [P, 2])
        neg_half = sb("neg_half", [P, M_TILES])
        neg_lam = sb("neg_lam", [P, 1])
        ms = sb("ms", [P, M_TILES])
        rstd = sb("rstd", [P, M_TILES])
        rstd_q = sb("rstd_q", [P, M_TILES])
        fl = sb("fl", [P, M_TILES, HEADS])
        fl_abs = sb("fl_abs", [P, M_TILES, HEADS])
        log_f = sb("log_f", [P, M_TILES, HEADS])
        c_nat = sb("c_nat", [P, M_TILES, HEADS])
        c_neg = sb("c_neg", [HEADS, SEQ])
        qkv_nat = sb("qkv_nat", [P, M_TILES, 3, HD])
        qk0T = sb("qk0T", [P, 2, P])
        qkT_hi = sb("qkT_hi", [P, 3 * P], fp32r)
        qkT_lo = sb("qkT_lo", [P, 3 * P], fp32r)
        bias = sb("bias", [P, 3 * P])
        probs = sb("probs", [P, 2, 3 * P])
        table_probe = sb("table_probe", [P, 1])
        wait_slot = sb("wait_slot", [P, 1])
        row_max = sb("row_max", [P, 4])
        neg_max = sb("neg_max", [P, 4])
        sums = sb("sums", [P, 4])
        inv = sb("inv", [P, 4])
        pT = sb("pT", [P, 3 * P])
        wfl_parts = sb("wfl_parts", [P, KT * 2 * HEADS + P - 2 * HEADS], fp32r)
        gate_tanh = sb("gate_tanh", [P, M_TILES, HD])
        gate = sb("gate", [P, M_TILES, HD])
        o_square = sb("o_square", [P, M_TILES, HD])
        og = sb("og", [P, M_TILES, HD])
        o_ssq = sb("o_ssq", [P, M_TILES])
        o_ms = sb("o_ms", [P, M_TILES])
        o_rstd = sb("o_rstd", [P, M_TILES])
        y_ssq = sb("y_ssq", [P, M_TILES, 5])
        y_part = sb("y_part", [P, M_TILES])
        last_hi = oT_hi[:].rearrange("p (t a) n -> p t (a n)", t=4).rearrange("p t (k n) -> p t k n", k=2)
        last_lo = oT_lo[:].rearrange("p (t a) n -> p t (a n)", t=4).rearrange("p t (k n) -> p t k n", k=2)
        early = diff_z[:, 1, :]
        wfl = early[:, 0:P].rearrange("p (k h) -> p k h", k=KT)
        lam_in = early[:, P:P + 4 * QK].rearrange("p (i d) -> p i d", i=4)
        lam_tmp = early[:, 3 * P:4 * P].rearrange("p (i d) -> p i d", i=2)
        ones = early[:, 4 * P:5 * P]
        gn_rows = early[0:KT, 5 * P:6 * P]
        flT = early[0:2 * HEADS, 6 * P:6 * P + SEQ]
        wfl_v = wfl_parts[:, 0:KT * 2 * HEADS].rearrange("p (k c) -> p k c", c=2 * HEADS)

        mask = consts[:, C_MASK:C_MASK + P]
        zero_mask = consts[:, C_ZERO:C_ZERO + 2 * P]
        tri = consts[:, C_TRI:C_TRI + P]
        cos = consts[:, C_COS:C_COS + 16].rearrange("p (m c) -> p m c", m=M_TILES)
        sin = consts[:, C_SIN:C_SIN + 16].rearrange("p (m c) -> p m c", m=M_TILES)
        sum_parts = consts[0:2 * HEADS, C_SEL:C_SEL + HEADS]
        x_sb = diff_z[:, 0, :].rearrange("p (m n) -> p m n", m=M_TILES)
        y_sb = diff_z[:, 1, :].rearrange("p (m n) -> p m n", m=M_TILES)
        m_a = diff_z[:, 1, 0:2 * CHUNK].rearrange("p (m n) -> p m n", m=M_TILES)
        m_b = diff_z[:, 1, 2 * CHUNK:4 * CHUNK].rearrange("p (m n) -> p m n", m=M_TILES)
        rope_t = fox_z[:, 0, 0:4 * 4 * HEADS * ROPE_HALF].rearrange("p (i b c) -> p i b c", i=4, c=ROPE_HALF)
        yg = fox_z[:, 0, :].rearrange("p (m n) -> p m n", m=M_TILES)
        square_out = fox_z[:, 1, :].rearrange("p (m n) -> p m n", m=M_TILES)

        Z = [bank(f"Z{i}") for i in range(4)]
        A, B, C, Dk = bank("A"), bank("B"), bank("C"), bank("Dk")
        T_BANKS = [A, B, C, Dk]

        LAST = ((0, slice(3 * CHUNK, 4 * CHUNK), Z[2]),
                (1, slice(3 * CHUNK, 7 * CHUNK // 2), Z[3]), (1, slice(7 * CHUNK // 2, 4 * CHUNK), A))
        ACT_OUT, DVE_OUT, LAST_OUT = slice(0, 3 * CHUNK // 2), slice(3 * CHUNK // 2, 3 * CHUNK), slice(3 * CHUNK, 4 * CHUNK)
        SMALL = 16 * 7

        raw_loaded = [sem(f"raw_loaded{i}") for i in range(RING)]
        hi_ready, lo_ready, w_used = sem("hi_ready"), sem("lo_ready"), sem("w_used")
        evac = [sem("evac0"), sem("evac1")]
        x_loaded = [sem(f"x_loaded{i}") for i in range(TILES)]
        ident_ready, gn_loaded, small_loaded = sem("ident_ready"), sem("gn_loaded"), sem("small_loaded")
        wfl_loaded = sem("wfl_loaded")
        gT_done, g_col_ready = sem("gT_done"), sem("g_col_ready")
        xT_done, xh_ready, xl_ready = sem("xT_done"), sem("xh_ready"), sem("xl_ready")
        x_squared, rstd_ready = sem("x_squared"), sem("rstd_ready")
        pool_const = sem("pool_const")
        wfl_hi_ready, wfl_ready = sem("wfl_hi_ready"), sem("wfl_ready")
        flT_done, flT_ready = sem("flT_done"), sem("flT_ready")
        fl_done, fl_ready, softplus_ready, log_f_ready = sem("fl_done"), sem("fl_ready"), sem("softplus_ready"), sem("log_f_ready")
        c_done, c_nat_ready, cT_done, c_neg_ready = sem("c_done"), sem("c_nat_ready"), sem("cT_done"), sem("c_neg_ready")
        c_stored, rows_loaded = sem("c_stored"), sem("rows_loaded")
        lam_dots, lam_exps = sem("lam_dots"), sem("lam_exps")
        act_step, dve_step, pool_step = sem("act_step"), sem("dve_step"), sem("pool_step")
        scale_ready, tanh_ready = sem("scale_ready"), sem("tanh_ready")
        qkv_ready, bias_ready = sem("qkv_ready"), sem("bias_ready")
        qkT_done, qkT_hi_ready, qkT_ready = sem("qkT_done"), sem("qkT_hi_ready"), sem("qkT_ready")
        scores_done, max_ready, exp_done, probs_ready = sem("scores_done"), sem("max_ready"), sem("exp_done"), sem("probs_ready")
        pT_done, pT_ready, o_done = sem("pT_done"), sem("pT_ready"), sem("o_done")
        o_ms_ready = sem("o_ms_ready")
        o_squared, o_rstd_ready, og_ready = sem("o_squared"), sem("o_rstd_ready"), sem("og_ready")
        oT_done, oT_hi_ready, oT_lo_ready = sem("oT_done"), sem("oT_hi_ready"), sem("oT_lo_ready")
        merge_tanh, m_ready, mT_done = sem("merge_tanh"), sem("m_ready"), sem("mT_done")
        mT_hi_ready, mT_lo_ready = sem("mT_hi_ready"), sem("mT_lo_ready")
        xres_loaded, gf_loaded = sem("xres_loaded"), sem("gf_loaded")
        y_squared, yg_ready = sem("y_squared"), sem("yg_ready")
        y_ms_ready, y_rstd_ready = sem("y_ms_ready"), sem("y_rstd_ready")
        out_ready, out_stored = [sem("out_ready0"), sem("out_ready1")], sem("out_stored")

        block = ctx.enter_context(nc.Block())

        @block.sync
        def _(sp):
            def load(c, j, src):
                if not (isinstance(c, int) and 8 * c + j < RING):
                    sp.wait_ge(lo_ready, 8 * c + (j - RING + 1))
                sp.dma_start(w_raw[:, j % RING], src).then_inc(raw_loaded[j % RING], 16)

            for j in range(TILES):
                sp.dma_start(x_sb[:, :, 2 * j * P:(2 * j + 2) * P], x_v[:, :, 2 * j * P:(2 * j + 2) * P]).then_inc(x_loaded[j], 16)
                load(0, j, w_in_v[:, 2 * j:2 * j + 2, FOX_COL:FOX_COL + CHUNK])
            with sp.Fori(1, 8) as c:
                for j in range(TILES):
                    load(c, j, w_in_v[:, 2 * j:2 * j + 2, ds(c * CHUNK + FOX_COL, CHUNK)])
            with sp.Fori(8, 16) as c:
                for j in range(TILES):
                    load(c, j, w_in_v[:, 2 * j:2 * j + 2, ds(c * CHUNK + (DIFF_COL - 8 * CHUNK), CHUNK)])
            with sp.Fori(16, 24) as c:
                for j in range(TILES):
                    load(c, j, w_in_v[:, 2 * j:2 * j + 2, ds(c * CHUNK + (MERGE_COL - 16 * CHUNK), CHUNK)])
            with sp.Fori(24, 28) as c:
                for j in range(TILES):
                    w = w_a_v if j < 4 else w_b_v
                    k = 2 * (j % 4)
                    load(c, j, w[:, k:k + 2, ds(c * CHUNK - 24 * CHUNK, CHUNK)])
            sp.wait_ge(oT_done, 2 * HEADS)
            sp.dma_start(x_sb, x_v).then_inc(xres_loaded, 16)
            sp.dma_start(rows[:], g_final.rearrange("(a n) -> a n", a=1).to_broadcast([P, D_MODEL])).then_inc(gf_loaded, 16)
            with sp.Fori(28, 32) as c:
                for j in range(TILES):
                    load(c, j, w_out_v[:, 2 * j:2 * j + 2, ds(c * CHUNK - 28 * CHUNK, CHUNK)])
            for m in range(M_TILES):
                for i, cols in enumerate((DVE_OUT, LAST_OUT)):
                    sp.wait_ge(out_ready[1], 2 * m + i + 1)
                    sp.dma_start(out_v[:, m, cols], yg[:, m, cols]).then_inc(out_stored, 16)
            sp.wait_ge(out_stored, 3 * M_TILES * 16)

        @block.tensor
        def _(pe):
            def split_product(acc, a_hi, a_lo, b_hi, b_lo, first, last):
                pe.matmul(acc, a_hi, b_hi, start=first, stop=False)
                pe.matmul(acc, a_hi, b_lo, start=False, stop=False)
                return pe.matmul(acc, a_lo, b_hi, start=False, stop=last)

            def tile(c, j, pair, stat_hi, stat_lo, k0, first, last):
                pe.wait_ge(hi_ready, 8 * c + (j + 1))
                pe.wait_ge(lo_ready, 8 * c + (j + 1))
                for kk in range(2):
                    for m in range(M_TILES):
                        tok = slice(m * P, (m + 1) * P)
                        mm = split_product(Z[2 * pair + m][:], stat_hi[:, k0 + kk, tok], stat_lo[:, k0 + kk, tok],
                                           w_hi[:, j % RING, kk], w_lo[:, j % RING, kk], first and kk == 0, last and kk == 1)
                mm.then_inc(w_used, 1)

            def banks_free(fill):
                pe.wait_ge(evac[0], fill - 1)
                pe.wait_ge(evac[1], fill - 1)

            def z_tile(c, j, pair):
                tile(c, j, pair, hT_hi, hT_lo, 2 * j, j == 0, j == TILES - 1)

            def x_transposes(j):
                pe.wait_ge(x_loaded[j], 16)
                if j == 3:
                    pe.wait_ge(g_col_ready, 1)
                if j >= 4:
                    pe.wait_ge(xl_ready, j - 3)
                for kk in range(2):
                    for m in range(M_TILES):
                        k = 2 * j + kk
                        mm = pe.transpose(T_BANKS[j % 4][:, (2 * kk + m) * P:(2 * kk + m + 1) * P],
                                          x_sb[:, m, k * P:(k + 1) * P], ident[:])
                mm.then_inc(xT_done, 1)

            def head_transposes(g):
                pe.wait_ge(qkv_ready, g + 1)
                for i in range(2):
                    for m in range(M_TILES):
                        mm = pe.transpose(A[:, (2 * i + m) * P:(2 * i + m + 1) * P], qkv_nat[:, m, i, :], ident[:])
                mm.then_inc(qkT_done, 1)

            def scores(g, maps):
                pe.wait_ge(qkT_ready, g + 1)
                for i in range(maps):
                    part = slice(0, P) if maps == 1 else slice(i * QK, (i + 1) * QK)
                    pe.matmul((B, C)[i][:, 0:P], qk0T[part, 0, :], qk0T[part, 1, :], start=True, stop=True)
                    mm = split_product((B, C)[i][:, P:3 * P], qkT_hi[part, 0:P], qkT_lo[part, 0:P],
                                       qkT_hi[part, P:3 * P], qkT_lo[part, P:3 * P], True, True)
                mm.then_inc(scores_done, 1)

            def prob_transposes(ready, count):
                pe.wait_ge(ready, count)
                for b in range(3):
                    mm = pe.transpose(Dk[:, b * P:(b + 1) * P], probs[:, 0, b * P:(b + 1) * P], ident[:])
                mm.then_inc(pT_done, 1)

            def values(g):
                pe.wait_ge(pT_ready, g + 1)
                for b, (q, k) in enumerate(((0, 0), (1, 0), (1, 1))):
                    mm = pe.matmul(A[:, q * P:(q + 1) * P], pT[:, b * P:(b + 1) * P], qkv_nat[:, k, 2, :],
                                   start=b < 2, stop=b != 1)
                mm.then_inc(o_done, 1)

            def gated_transposes(g):
                pe.wait_ge(og_ready, g + 1)
                for m in range(M_TILES):
                    mm = pe.transpose(Dk[:, m * P:(m + 1) * P], og[:, m, :], ident[:])
                mm.then_inc(oT_done, 1)

            def merged_transposes(n):
                pe.wait_ge(m_ready, n + 1)
                for i in range(4):
                    for m in range(M_TILES):
                        mm = pe.transpose((A, B)[i // 2][:, (2 * (i % 2) + m) * P:(2 * (i % 2) + m + 1) * P],
                                          m_a[:, m, i * P:(i + 1) * P], ident[:])
                mm.then_inc(mT_done, 1)

            pe.wait_ge(ident_ready, 2)
            pe.wait_ge(gn_loaded, 16)
            pe.matmul(Dk[:, 0:KT], gn_rows, ident[0:KT, 0:KT], start=True, stop=True).then_inc(gT_done, 1)
            x_transposes(0)
            for j in range(TILES):
                for part, (x_part, w_part) in enumerate(((hT_hi, w_hi), (hT_lo, w_hi), (hT_hi, w_lo))):
                    if part == 0:
                        pe.wait_ge(xh_ready, j + 1)
                        pe.wait_ge(hi_ready, j + 1)
                    if part == 1:
                        pe.wait_ge(xl_ready, j + 1)
                    if part == 2:
                        pe.wait_ge(lo_ready, j + 1)
                    for kk in range(2):
                        for m in range(M_TILES):
                            mm = pe.matmul(Z[m][:], x_part[:, 2 * j + kk, m * P:(m + 1) * P], w_part[:, j % RING, kk],
                                           start=(j == 0 and part == 0 and kk == 0),
                                           stop=(j == TILES - 1 and part == 2 and kk == 1))
                    if part == 0 and j == 0:
                        x_transposes(1)
                    if part == 1 and j + 2 < TILES:
                        x_transposes(j + 2)
                mm.then_inc(w_used, 1)
            for j in range(TILES):
                z_tile(1, j, 1)
                if j == 1:
                    pe.wait_ge(wfl_ready, 3)
                    for k in range(KT):
                        for n, part in enumerate((hT_hi, hT_lo)):
                            mm = pe.matmul(A[:, 0:SEQ], wfl_parts[:, 2 * HEADS * k:2 * HEADS * k + P], part[:, k, :],
                                           start=(k == 0 and n == 0), stop=(k == KT - 1 and n == 1))
                    mm.then_inc(flT_done, 1)
                if j == 2:
                    pe.wait_ge(flT_ready, 1)
                    pe.wait_ge(small_loaded, SMALL)
                    for m in range(M_TILES):
                        mm = pe.matmul(B[:, m * HEADS:(m + 1) * HEADS], flT[:, m * P:(m + 1) * P], sum_parts, start=True, stop=True)
                    mm.then_inc(fl_done, 1)
                if j == 4:
                    pe.wait_ge(log_f_ready, 1)
                    pe.wait_ge(pool_const, 1)
                    pe.matmul(B[:, 0:HEADS], tri, log_f[:, 0, :], start=True, stop=True)
                    pe.matmul(B[:, HEADS:2 * HEADS], ones, log_f[:, 0, :], start=True, stop=False)
                    pe.matmul(B[:, HEADS:2 * HEADS], tri, log_f[:, 1, :], start=False, stop=True).then_inc(c_done, 1)
                if j == 6:
                    pe.wait_ge(c_nat_ready, 1)
                    for m in range(M_TILES):
                        mm = pe.matmul(C[0:HEADS, m * P:(m + 1) * P], c_nat[:, m, :], ident[:], start=True, stop=True)
                    mm.then_inc(cT_done, 1)

            with pe.Fori(1, 4) as i:
                for half in range(2):
                    c = 2 * i + half
                    banks_free(c)
                    for j in range(TILES):
                        z_tile(c, j, half)
            with pe.Fori(4, 8) as i:
                for half in range(2):
                    c = 2 * i + half
                    banks_free(c)
                    for j in range(TILES):
                        z_tile(c, j, half)
                        if j == 0:
                            head_transposes(c - 8)
                        if j == 1:
                            scores(c - 8, 1)
                        if j == 4:
                            prob_transposes(exp_done, c - 7)
                        if j == 5:
                            values(c - 8)
                        if j == 7:
                            gated_transposes(c - 8)
            with pe.Fori(8, 12) as i:
                for half in range(2):
                    c = 2 * i + half
                    banks_free(c)
                    for j in range(TILES):
                        z_tile(c, j, half)
                        if j == 0:
                            head_transposes(c - 8)
                        if j == 1:
                            scores(c - 8, 2)
                        if j == 4:
                            prob_transposes(probs_ready, c - 15)
                        if j == 5:
                            values(c - 8)
                        if j == 7:
                            gated_transposes(c - 8)

            def projection(n):
                for j in range(TILES):
                    if j % 4 == 0:
                        banks_free(2 * n + (24 + j // 4))
                    if j < 4 and isinstance(n, int):
                        pe.wait_ge(oT_lo_ready, HEADS + 2 * j + 2)
                    tile(n + 24, j, j // 4, oT_hi, oT_lo, (HEADS if j < 4 else 0) + 2 * (j % 4), j % 4 == 0, j % 4 == 3)
                    if j == 1 and not isinstance(n, int):
                        merged_transposes(n - 1)

            projection(0)
            with pe.Fori(1, 4) as n:
                projection(n)
            for n in range(3):
                c = 28 + n
                banks_free(32 + n)
                for j in range(TILES):
                    if n == 0:
                        pe.wait_ge(mT_lo_ready, j + 1)
                    z_tile(c, j, n % 2)
                    if n == 0 and j == 1:
                        merged_transposes(3)
            banks_free(35)
            for part, (m, y_cols, acc) in enumerate(LAST):
                tok = slice(m * P, (m + 1) * P)
                n = y_cols.stop - y_cols.start
                cols = slice(y_cols.start - 3 * CHUNK, y_cols.stop - 3 * CHUNK)
                for j in range(TILES):
                    if part == 0:
                        pe.wait_ge(hi_ready, 8 * 31 + j + 1)
                        pe.wait_ge(lo_ready, 8 * 31 + j + 1)
                    hi, lo = (last_hi[:, j], last_lo[:, j]) if j < 4 else (w_hi[:, j % RING], w_lo[:, j % RING])
                    for kk in range(2):
                        k = 2 * j + kk
                        mm = split_product(acc[:, 0:n], hT_hi[:, k, tok], hT_lo[:, k, tok], hi[:, kk, cols],
                                           lo[:, kk, cols], k == 0, k == KT - 1)
                mm.then_inc(w_used, 1)

        @block.scalar
        def _(act):
            def split(c, j):
                act.wait_ge(w_used, 8 * c + (j + 1))
                act.wait_ge(raw_loaded[j % RING], 32 * c + (16 * (2 + (j >= 4))))
                act.activation(w_hi[:, j % RING], w_raw[:, j % RING], ACT.Copy).then_inc(hi_ready, 1)

            def evacuate(c, half, z, col, factor=rstd):
                act.wait_ge(w_used, 8 * c + 8)
                act.activation(z[:, 0, ds(col, CHUNK)], Z[2 * half][:], ACT.Copy, scale=factor[:, 0:1]).then_inc(evac[0], 1)

            def x_part(j):
                act.wait_ge(xT_done, j + 1)
                for kk in range(2):
                    k = 2 * j + kk
                    ins = act.activation(hT_hi[:, k, :], T_BANKS[j % 4][:, kk * SEQ:(kk + 1) * SEQ], ACT.Copy,
                                         scale=g_col[:, k:k + 1])
                ins.then_inc(xh_ready, 1)

            act.dma_start(gn_rows, g_norm[0].rearrange("(k p) -> k p", p=P)).then_inc(gn_loaded, 16)
            act.wait_ge(scale_ready, 1)
            act.activation(table_probe[:], o_scale[:, 0:1], ACT.Copy)
            act.wait_ge(g_col_ready, 1)
            for j in range(RING):
                x_part(j)
                if j > 0:
                    act.wait_ge(hi_ready, j)
                    act.wait_ge(raw_loaded[j], 16)
                    act.activation(w_hi[:, j], w_raw[:, j], ACT.Copy).then_inc(hi_ready, 1)
            for j in range(TILES):
                if j < 4:
                    x_part(j + 4)
                if j == 4:
                    act.wait_ge(wfl_loaded, 16)
                    act.activation(wfl_v[:, :, 0:HEADS], wfl, ACT.Copy).then_inc(wfl_hi_ready, 1)
                if j in (5, 6):
                    m = j - 5
                    act.activation(square_out[:, m, :], x_sb[:, m, :], ACT.Square, scale=D_MODEL ** -0.5,
                                   accum_out=ms[:, m:m + 1]).then_inc(x_squared, 1)
                split(0, j)
            act.wait_ge(rstd_ready, 2)
            evacuate(0, 0, fox_z, 0, rstd_q)
            for j in range(TILES):
                if j == 2:
                    act.wait_ge(fl_ready, 1)
                    act.activation(fl_abs[:], fl[:], ACT.Abs).then_inc(act_step, 1)
                    act.wait_ge(act_step, 1)
                    act.activation(fl_abs[:], fl_abs[:], ACT.Exp, scale=-1.0).then_inc(act_step, 1)
                    act.wait_ge(act_step, 2)
                    act.activation(fl_abs[:], fl_abs[:], ACT.Ln, bias=1.0).then_inc(softplus_ready, 1)
                if j == 6:
                    act.wait_ge(lam_dots, 2)
                    act.activation(lam_exp[:], lam_dot[:], ACT.Exp).then_inc(lam_exps, 1)
                split(1, j)
            evacuate(1, 1, fox_z, CHUNK, rstd_q)
            with act.Fori(1, 4) as i:
                for half in range(2):
                    c = 2 * i + half
                    for j in range(TILES):
                        split(c, j)
                    evacuate(c, half, fox_z, c * CHUNK)

            def head_qkT(g):
                act.wait_ge(qkT_done, g + 1)
                act.activation(qk0T[:], A[:].rearrange("p (i n) -> p i n", i=2)[:, :, 0:P], ACT.Copy)
                act.activation(qkT_hi[:], A[:, P:4 * P], ACT.Copy).then_inc(qkT_hi_ready, 1)

            def head_pT(g):
                act.wait_ge(pT_done, g + 1)
                act.activation(pT[:], Dk[:, 0:3 * P], ACT.Copy).then_inc(pT_ready, 1)

            def tanh(z, h, n):
                act.wait_ge(evac[0], n)
                act.wait_ge(evac[1], n)
                act.activation(gate_tanh[:], z[:, :, ds(h * HD + G_OFF, HD)], ACT.Tanh, scale=0.5).then_inc(tanh_ready, 1)

            def exps(g, maps, scale):
                act.wait_ge(max_ready, g + 1)
                for i in range(maps):
                    act.activation(probs[:, i, 0:P], probs[:, i, 0:P], ACT.Exp, bias=neg_max[:, 2 * i:2 * i + 1],
                                   scale=scale, accum_out=sums[:, 2 * i:2 * i + 1])
                    ins = act.activation(probs[:, i, P:3 * P], probs[:, i, P:3 * P], ACT.Exp,
                                         bias=neg_max[:, 2 * i + 1:2 * i + 2], scale=scale,
                                         accum_out=sums[:, 2 * i + 1:2 * i + 2])
                ins.then_inc(exp_done, 1)

            def gated_hi(g, branch):
                act.wait_ge(oT_done, g + 1)
                act.activation(oT_hi[:, ds(g, 1), :], Dk[:, 0:SEQ].rearrange("p (a n) -> p a n", a=1), ACT.Copy,
                               scale=o_scale[:, branch:branch + 1]).then_inc(oT_hi_ready, 1)

            act.wait_ge(scale_ready, 2)
            with act.Fori(4, 8) as i:
                for half in range(2):
                    c = 2 * i + half
                    for j in range(TILES):
                        if j == 0:
                            head_qkT(c - 8)
                        if j == 4:
                            head_pT(c - 8)
                        if j == 7:
                            gated_hi(c - 8, 0)
                        split(c, j)
                        if j == 1:
                            exps(c - 8, 1, 1.0)
                        if j == 2:
                            tanh(fox_z, c - 8, 8)
                    evacuate(c, half, diff_z, c * CHUNK - 8 * CHUNK)
            with act.Fori(8, 12) as i:
                for half in range(2):
                    c = 2 * i + half
                    for j in range(TILES):
                        if j == 0:
                            head_qkT(c - 8)
                        if j == 4:
                            head_pT(c - 8)
                        if j == 5:
                            act.wait_ge(o_done, c - 7)
                            for m in range(M_TILES):
                                ins = act.activation(o_square[:, m, :], A[:, m * P:(m + 1) * P], ACT.Square,
                                                     accum_out=o_ssq[:, m:m + 1])
                            ins.then_inc(o_squared, 1)
                        if j == 7:
                            gated_hi(c - 8, 1)
                        split(c, j)
                        if j == 1:
                            exps(c - 8, 2, QK ** -0.5)
                        if j == 2:
                            tanh(diff_z, c - 16, 16)
                    evacuate(c, half, fox_z, c * CHUNK - 16 * CHUNK)

            def merged_hi(n):
                act.wait_ge(mT_done, n + 1)
                for b in range(2):
                    act.activation(hT_hi[:, ds(4 * n + 2 * b, 2), :], (A, B)[b][:].rearrange("p (a n) -> p a n", a=2),
                                   ACT.Copy, scale=0.5).then_inc(mT_hi_ready, 1)

            def projection(n):
                for j in range(TILES):
                    if j < 2:
                        z = fox_z[:, :, ds(n * CHUNK + j * D_MODEL, CHUNK)]
                        act.activation(z, z, ACT.Tanh, scale=0.5).then_inc(merge_tanh, 1)
                    if j == 2 and not isinstance(n, int):
                        merged_hi(n - 1)
                    split(n + 24, j)

            act.wait_ge(evac[1], 24)
            act.wait_ge(evac[0], 24)
            projection(0)
            with act.Fori(1, 4) as n:
                projection(n)
            def square(m, piece, cols, residuals):
                act.wait_ge(evac[m], residuals)
                act.activation(square_out[:, m, cols], y_sb[:, m, cols], ACT.Square, scale=D_MODEL ** -0.5,
                               accum_out=y_ssq[:, m, piece:piece + 1]).then_inc(y_squared, 1)

            for n in range(3):
                for j in range(TILES):
                    if n == 0 and j == 2:
                        merged_hi(3)
                    if n == 2 and j >= 4:
                        act.wait_ge(raw_loaded[j % RING], 16 * 63)
                        act.activation(last_hi[:, j - 4], w_raw[:, j % RING], ACT.Copy).then_inc(hi_ready, 1)
                    else:
                        split(28 + n, j)
                for m in range(M_TILES):
                    square(m, n, slice(n * CHUNK, (n + 1) * CHUNK), 33 + n)
            for j in range(4, TILES):
                act.wait_ge(w_used, 8 * 30 + j + 1)
                act.wait_ge(raw_loaded[j % RING], 16 * 64)
                act.activation(w_hi[:, j % RING], w_raw[:, j % RING], ACT.Copy).then_inc(hi_ready, 1)
            for part, (m, cols, _) in enumerate(LAST):
                piece = 4 if part == 2 else 3
                square(m, piece, cols, 33 + piece)
                if part == 1:
                    continue
                act.wait_ge(yg_ready, 6)
                act.wait_ge(y_rstd_ready, m + 1)
                act.activation(yg[:, m, ACT_OUT], yg[:, m, ACT_OUT], ACT.Copy, scale=rstd[:, m:m + 1]).then_inc(out_ready[0], 1)
                act.wait_ge(out_ready[0], m + 1)
                act.dma_start(out_v[:, m, ACT_OUT], yg[:, m, ACT_OUT]).then_inc(out_stored, 16)

        @block.vector
        def _(dve):
            step = [0]

            def chained(ins):
                step[0] += 1
                ins.then_inc(dve_step, 1)
                dve.wait_ge(dve_step, step[0])

            def split(c, j):
                dve.wait_ge(hi_ready, 8 * c + (j + 5))
                dve.tensor_tensor(w_lo[:, j % RING], w_raw[:, j % RING], w_hi[:, j % RING].bitcast(fp32),
                                  ALU.subtract).then_inc(lo_ready, 1)

            def evacuate(c, half, z, col, factor=rstd):
                dve.wait_ge(w_used, 8 * c + 8)
                dve.tensor_scalar(z[:, 1, ds(col, CHUNK)], Z[2 * half + 1][:], factor[:, 1:2], None,
                                  ALU.mult).then_inc(evac[1], 1)

            def x_part(j):
                dve.wait_ge(xh_ready, j + 1)
                for kk in range(2):
                    k = 2 * j + kk
                    ins = dve.scalar_tensor_tensor(hT_lo[:, k, :], T_BANKS[j % 4][:, kk * SEQ:(kk + 1) * SEQ],
                                                   g_col[:, k:k + 1], hT_hi[:, k, :].bitcast(fp32), ALU.mult, ALU.subtract)
                ins.then_inc(xl_ready, 1)

            dve.memset(wfl_parts[:, KT * 2 * HEADS:].bitcast(fp32), 0.0).then_inc(wfl_ready, 1)
            dve.memset(o_scale[:, 0:1], 0.5).then_inc(scale_ready, 1)
            dve.wait_ge(gT_done, 1)
            dve.tensor_copy(g_col[:], Dk[:, 0:KT]).then_inc(g_col_ready, 1)
            dve.wait_ge(raw_loaded[0], 16)
            dve.tensor_copy(w_hi[:, 0], w_raw[:, 0]).then_inc(hi_ready, 1)
            for j in range(RING):
                x_part(j)
                dve.wait_ge(hi_ready, j + 1)
                dve.tensor_tensor(w_lo[:, j], w_raw[:, j], w_hi[:, j].bitcast(fp32), ALU.subtract).then_inc(lo_ready, 1)
            for j in range(TILES):
                if j < 4:
                    x_part(j + 4)
                if j == 5:
                    dve.wait_ge(wfl_hi_ready, 1)
                    dve.tensor_tensor(wfl_v[:, :, HEADS:2 * HEADS], wfl, wfl_v[:, :, 0:HEADS].bitcast(fp32),
                                      ALU.subtract).then_inc(wfl_ready, 2)
                split(0, j)
            dve.wait_ge(rstd_ready, 2)
            evacuate(0, 0, fox_z, 0, rstd_q)
            for j in range(TILES):
                if j == 1:
                    dve.wait_ge(flT_done, 1)
                    dve.tensor_copy(flT, A[0:2 * HEADS, 0:SEQ]).then_inc(flT_ready, 1)
                if j == 2:
                    dve.wait_ge(fl_done, 1)
                    dve.wait_ge(small_loaded, SMALL)
                    for m in range(M_TILES):
                        ins = dve.scalar_tensor_tensor(fl[:, m, :], B[:, m * HEADS:(m + 1) * HEADS], rstd[:, m:m + 1], b_row[:],
                                                       ALU.mult, ALU.add)
                    ins.then_inc(fl_ready, 1)
                if j == 3:
                    dve.wait_ge(softplus_ready, 1)
                    dve.scalar_tensor_tensor(log_f[:], fl[:], 0.0, fl_abs[:], ALU.min, ALU.subtract).then_inc(log_f_ready, 1)
                if j == 4:
                    dve.wait_ge(c_done, 1)
                    dve.tensor_copy(c_nat[:].rearrange("p m h -> p (m h)"), B[:, 0:2 * HEADS]).then_inc(c_nat_ready, 1)
                if j == 6:
                    dve.wait_ge(cT_done, 1)
                    dve.tensor_scalar(c_neg[:], C[0:HEADS, 0:SEQ], -1.0, None, ALU.mult).then_inc(c_neg_ready, 1)
                if j == 5:
                    for i in range(2):
                        dve.tensor_tensor_reduce(lam_tmp[:, i], lam_in[:, 2 * i, :], lam_in[:, 2 * i + 1, :], 1.0, 0.0,
                                                 ALU.mult, ALU.add, lam_dot[:, i:i + 1]).then_inc(lam_dots, 1)
                if j == 7:
                    dve.wait_ge(lam_exps, 1)
                    chained(dve.tensor_tensor(neg_lam[:], lam_exp[:, 1:2], lam_exp[:, 0:1], ALU.subtract))
                    dve.tensor_scalar(neg_lam[:], neg_lam[:], -LAM_INIT, None, ALU.add)
                    dve.tensor_scalar(o_scale[:, 1:2], o_scale[:, 1:2], 0.5 * (1.0 - LAM_INIT), None, ALU.mult).then_inc(scale_ready, 1)
                split(1, j)
            evacuate(1, 1, fox_z, CHUNK, rstd_q)
            with dve.Fori(1, 4) as i:
                for half in range(2):
                    c = 2 * i + half
                    for j in range(TILES):
                        split(c, j)
                    evacuate(c, half, fox_z, c * CHUNK)

            def masked_max(S, i, add0, add1):
                if i == 0:
                    dve.memset(wait_slot[:], 0.0)
                dve.tensor_tensor_reduce(probs[:, i, 0:P], S[:, 0:P], add0, 1.0, NEG, ALU.add, ALU.max,
                                         row_max[:, 2 * i:2 * i + 1]).then_inc(dve_step, 1)
                dve.tensor_tensor_reduce(probs[:, i, P:3 * P], S[:, P:3 * P], add1, 1.0, NEG, ALU.add, ALU.max,
                                         row_max[:, 2 * i + 1:2 * i + 2]).then_inc(dve_step, 1)

            def head_qkT_lo(g):
                dve.wait_ge(qkT_hi_ready, g + 1)
                dve.tensor_tensor(qkT_lo[:], A[:, P:4 * P], qkT_hi[:].bitcast(fp32), ALU.subtract).then_inc(qkT_ready, 1)

            def gate_product(z, h, g):
                dve.wait_ge(tanh_ready, g + 1)
                dve.scalar_tensor_tensor(gate[:], gate_tanh[:], 1.0, z[:, :, ds(h * HD + G_OFF, HD)],
                                         ALU.add, ALU.mult).then_inc(dve_step, 1)

            def gated_lo(g, branch):
                dve.wait_ge(oT_hi_ready, g + 1)
                dve.scalar_tensor_tensor(oT_lo[:, ds(g, 1), :], Dk[:, 0:SEQ].rearrange("p (a n) -> p a n", a=1),
                                         o_scale[:, branch:branch + 1], oT_hi[:, ds(g, 1), :].bitcast(fp32),
                                         ALU.mult, ALU.subtract).then_inc(oT_lo_ready, 1)

            s0 = step[0]
            with dve.Fori(4, 8) as i:
                for half in range(2):
                    c = 2 * i + half
                    steps = 3 * c + (s0 - 24)
                    for j in range(TILES):
                        if j == 0:
                            head_qkT_lo(c - 8)
                        if j == 1:
                            dve.wait_ge(scores_done, c - 7)
                            dve.wait_ge(bias_ready, 2 * c - 14)
                            masked_max(B, 0, bias[:, 0:P], bias[:, P:3 * P])
                            dve.wait_ge(dve_step, steps + 2)
                            dve.tensor_scalar(neg_max[:, 0:2], row_max[:, 0:2], -1.0, None, ALU.mult).then_inc(max_ready, 1)
                        if j == 3:
                            dve.wait_ge(exp_done, c - 7)
                            dve.reciprocal(inv[:, 0:2], sums[:, 0:2])
                            gate_product(fox_z, c - 8, c - 8)
                        if j == 5:
                            dve.wait_ge(o_done, c - 7)
                            dve.wait_ge(dve_step, steps + 3)
                            for m in range(M_TILES):
                                ins = dve.scalar_tensor_tensor(og[:, m, :], A[:, m * P:(m + 1) * P], inv[:, m:m + 1],
                                                               gate[:, m, :], ALU.mult, ALU.mult)
                            ins.then_inc(og_ready, 1)
                        if j == 7:
                            gated_lo(c - 8, 0)
                        split(c, j)
                    evacuate(c, half, diff_z, c * CHUNK - 8 * CHUNK)
            s1 = s0 + 3 * HEADS
            with dve.Fori(8, 12) as i:
                for half in range(2):
                    c = 2 * i + half
                    steps = 9 * c + (s1 - 144)
                    for j in range(TILES):
                        if j == 0:
                            head_qkT_lo(c - 8)
                        if j == 1:
                            dve.wait_ge(scores_done, c - 7)
                            for mp, S in enumerate((B, C)):
                                masked_max(S, mp, mask, zero_mask)
                            dve.wait_ge(dve_step, steps + 4)
                            dve.tensor_scalar(neg_max[:], row_max[:], -(QK ** -0.5), None, ALU.mult).then_inc(max_ready, 1)
                        if j == 2:
                            dve.wait_ge(exp_done, c - 7)
                            dve.reciprocal(inv[:], sums[:]).then_inc(dve_step, 1)
                            dve.wait_ge(dve_step, steps + 5)
                            dve.tensor_scalar(inv[:, 2:4], inv[:, 2:4], neg_lam[:, 0:1], None, ALU.mult).then_inc(dve_step, 1)
                            dve.wait_ge(dve_step, steps + 6)
                            for m, sl in enumerate((slice(0, P), slice(P, 3 * P))):
                                dve.tensor_scalar(probs[:, 1, sl], probs[:, 1, sl], inv[:, 2 + m:3 + m], None,
                                                  ALU.mult).then_inc(dve_step, 1)
                            dve.wait_ge(dve_step, steps + 8)
                            for m, sl in enumerate((slice(0, P), slice(P, 3 * P))):
                                ins = dve.scalar_tensor_tensor(probs[:, 0, sl], probs[:, 0, sl], inv[:, m:m + 1],
                                                               probs[:, 1, sl], ALU.mult, ALU.add)
                            ins.then_inc(probs_ready, 1)
                        if j == 3:
                            gate_product(diff_z, c - 16, c - 8)
                        if j == 5:
                            dve.wait_ge(o_squared, c - 15)
                            dve.tensor_scalar(o_ms[:], o_ssq[:], 1.0 / HD, EPS, ALU.mult, ALU.add).then_inc(o_ms_ready, 1)
                        if j == 6:
                            dve.wait_ge(o_rstd_ready, c - 15)
                            dve.wait_ge(dve_step, steps + 9)
                            for m in range(M_TILES):
                                ins = dve.scalar_tensor_tensor(og[:, m, :], A[:, m * P:(m + 1) * P], o_rstd[:, m:m + 1],
                                                               gate[:, m, :], ALU.mult, ALU.mult)
                            ins.then_inc(og_ready, 1)
                        if j == 7:
                            gated_lo(c - 8, 1)
                        split(c, j)
                    evacuate(c, half, fox_z, c * CHUNK - 16 * CHUNK)

            def merged_lo(n):
                for b in range(2):
                    dve.wait_ge(mT_hi_ready, 2 * n + (b + 1))
                    dve.scalar_tensor_tensor(hT_lo[:, ds(4 * n + 2 * b, 2), :], (A, B)[b][:].rearrange("p (a n) -> p a n", a=2),
                                             0.5, hT_hi[:, ds(4 * n + 2 * b, 2), :].bitcast(fp32),
                                             ALU.mult, ALU.subtract).then_inc(mT_lo_ready, 1)

            def gate_branch(n, branch, dst):
                dve.wait_ge(w_used, 8 * n + (8 * 24 + 4 + 4 * branch))
                dve.wait_ge(merge_tanh, 2 * n + (1 + branch))
                for m in range(M_TILES):
                    dve.scalar_tensor_tensor(dst[:, m, :], fox_z[:, m, ds(n * CHUNK + branch * D_MODEL, CHUNK)], 1.0,
                                             Z[2 * branch + m][:], ALU.add, ALU.mult).then_inc(evac[m], 1)

            def projection(n):
                for j in range(TILES):
                    if j == 2 and not isinstance(n, int):
                        merged_lo(n - 1)
                    split(n + 24, j)
                    if j == 3:
                        gate_branch(n, 0, m_a)
                gate_branch(n, 1, m_b)
                dve.wait_ge(evac[1], 2 * n + 26)
                dve.tensor_tensor(m_a, m_a, m_b, ALU.add).then_inc(m_ready, 1)

            projection(0)
            with dve.Fori(1, 4) as n:
                projection(n)
            dve.wait_ge(xres_loaded, 16)

            def residual(m, n):
                sl = slice(n * CHUNK, (n + 1) * CHUNK)
                dve.tensor_tensor(y_sb[:, m, sl], Z[2 * (n % 2) + m][:], x_sb[:, m, sl], ALU.add).then_inc(evac[m], 1)

            for n in range(3):
                for j in range(TILES):
                    if n == 0 and j == 2:
                        merged_lo(3)
                    if n == 2 and j >= 4:
                        dve.wait_ge(hi_ready, 8 * 31 + j - 3)
                        dve.tensor_tensor(last_lo[:, j - 4], w_raw[:, j % RING], last_hi[:, j - 4].bitcast(fp32),
                                          ALU.subtract).then_inc(lo_ready, 1)
                    else:
                        split(28 + n, j)
                dve.wait_ge(w_used, 8 * (29 + n))
                for m in range(M_TILES):
                    residual(m, n)
            for j in range(4):
                split(31, j)
            dve.wait_ge(gf_loaded, 16)
            dve.wait_ge(y_squared, 6)
            dve.tensor_reduce(ms[:], y_ssq[:, :, 0:3], AX.X, ALU.add).then_inc(y_ms_ready, 1)
            dve.wait_ge(y_ms_ready, 1)
            dve.tensor_scalar(y_part[:], ms[:], EPS, None, ALU.add).then_inc(y_ms_ready, 1)
            for part, (m, cols, acc) in enumerate(LAST):
                dve.wait_ge(w_used, 8 * 31 + part + 1)
                dve.tensor_tensor(y_sb[:, m, cols], acc[:, 0:cols.stop - cols.start], x_sb[:, m, cols],
                                  ALU.add).then_inc(evac[m], 1)
                dve.wait_ge(y_squared, 7 + part)
                dve.wait_ge(y_ms_ready, 2 + part)
                if part == 1:
                    dve.tensor_tensor(y_part[:, 1:2], y_ssq[:, 1, 3:4], y_part[:, 1:2], ALU.add).then_inc(y_ms_ready, 1)
                    continue
                dve.tensor_tensor(ms[:, m:m + 1], y_ssq[:, m, 3 + m:4 + m], y_part[:, m:m + 1], ALU.add).then_inc(y_ms_ready, 1)
                dve.wait_ge(y_rstd_ready, m + 1)
                dve.wait_ge(yg_ready, 6)
                dve.tensor_scalar(yg[:, m, DVE_OUT], yg[:, m, DVE_OUT], rstd[:, m:m + 1], None, ALU.mult).then_inc(out_ready[1], 1)
                dve.wait_ge(evac[m], 36 + m)
                dve.scalar_tensor_tensor(yg[:, m, LAST_OUT], y_sb[:, m, LAST_OUT], rstd[:, m:m + 1], rows[:, LAST_OUT],
                                         ALU.mult, ALU.mult).then_inc(out_ready[1], 1)

        @block.gpsimd
        def _(pool):
            step = [0]

            def chained(ins):
                step[0] += 1
                ins.then_inc(pool_step, 1)
                pool.wait_ge(pool_step, step[0])

            pool.memset(ident[:], 0.0).then_inc(ident_ready, 1)
            pool.wait_ge(ident_ready, 1)
            pool.affine_select(out=ident[:], in_=ident[:], compare_op=ALU.not_equal, fill=1.0, base=0,
                               pattern=[[-1, P]], channel_multiplier=1).then_inc(ident_ready, 1)
            pool.dma_start(o_scale[:, 1:2], g_subln.rearrange("a d -> d a")).then_inc(small_loaded, 16)
            pool.dma_start(b_row[:], b_forget.to_broadcast([P, HEADS])).then_inc(small_loaded, 16)
            pool.dma_start(wfl, w_in_v[:, :, FL_COL:FL_COL + HEADS]).then_inc(wfl_loaded, 16)
            for i, v in enumerate((lq1, lk1, lq2, lk2)):
                pool.dma_start(lam_in[:, i, :], v.to_broadcast([P, QK])).then_inc(small_loaded, 16)
            pool.dma_start(consts[:], consts_in).then_inc(small_loaded, 16)
            pool.memset(ones, 1.0).then_inc(pool_const, 1)
            pool.memset(neg_half[:], -0.5).then_inc(pool_const, 1)
            pool.wait_ge(pool_const, 2)
            pool.wait_ge(x_squared, 2)
            chained(pool.tensor_scalar(ms[:], ms[:], EPS, None, ALU.add))
            pool.tensor_tensor(rstd[:], ms[:], neg_half[:], ALU.pow).then_inc(rstd_ready, 1)
            pool.wait_ge(rstd_ready, 1)
            pool.tensor_scalar(rstd_q[:], rstd[:], HD ** -0.5, None, ALU.mult).then_inc(rstd_ready, 1)
            pool.wait_ge(c_neg_ready, 1)
            pool.dma_start(c_rows_dram, c_neg[:]).then_inc(c_stored, 16)
            pool.wait_ge(c_stored, 16)
            pool.dma_start(rows[:], c_rows_dram.rearrange("(a h) n -> a (h n)", a=1).to_broadcast([P, HEADS * SEQ])).then_inc(rows_loaded, 16)

            def past(c):
                pool.wait_ge(w_used, 8 * c - 1)

            def head_copy(z, h):
                src = z[:, :, 0:3 * WIDTH].rearrange("p m (i n) -> p m i n", i=3)[:, :, :, ds(h * HD, HD)]
                pool.tensor_copy(qkv_nat[:], src).then_inc(qkv_ready, 1)

            def head_bias(h, steps):
                for m, sl in enumerate((slice(0, P), slice(P, 3 * P))):
                    n = (m + 1) * P
                    pool.tensor_tensor(bias[:, sl], rows[:].rearrange("p (h n) -> p h n", h=HEADS)[:, ds(h, 1), 0:n],
                                       c_nat[:, m, ds(h, 1)].unsqueeze(2).to_broadcast([P, 1, n]),
                                       ALU.add).then_inc(pool_step, 1)
                pool.wait_ge(pool_step, steps)
                for sl in (slice(0, P), slice(2 * P, 3 * P)):
                    pool.tensor_tensor(bias[:, sl], bias[:, sl], mask, ALU.add).then_inc(bias_ready, 1)

            def evacuated(n):
                pool.wait_ge(evac[0], n)
                pool.wait_ge(evac[1], n)

            evacuated(6)
            pool.wait_ge(rows_loaded, 16)
            pool.wait_ge(c_nat_ready, 1)
            head_copy(fox_z, 0)
            head_bias(0, step[0] + 2)
            with pool.Fori(9, 16) as c:
                past(c)
                head_copy(fox_z, c - 8)
                head_bias(c - 8, 2 * c + (step[0] + 2 - 16))
            step[0] += 2 * HEADS

            evacuated(12)
            for m in range(M_TILES):
                blocks = diff_z[:, m, 0:2 * WIDTH].rearrange("p (b d) -> p b d", d=QK)
                x1, x2 = blocks[:, :, 0:ROPE_HALF], blocks[:, :, ROPE_HALF:2 * ROPE_HALF]
                shape = [P, 2 * 2 * HEADS, ROPE_HALF]
                cos_m, sin_m = (t[:, m, :].unsqueeze(1).to_broadcast(shape) for t in (cos, sin))
                for i, (u, v) in enumerate(((x1, cos_m), (x2, sin_m), (x2, cos_m), (x1, sin_m))):
                    ins = pool.tensor_tensor(rope_t[:, i], u, v, ALU.mult)
                chained(ins)
                pool.tensor_tensor(x1, rope_t[:, 0], rope_t[:, 1], ALU.subtract)
                chained(pool.tensor_tensor(x2, rope_t[:, 2], rope_t[:, 3], ALU.add))
            evacuated(14)
            past(16)
            head_copy(diff_z, 0)

            def head_rstd(c):
                pool.wait_ge(o_ms_ready, c - 15)
                pool.tensor_tensor(o_rstd[:], o_ms[:], neg_half[:], ALU.pow).then_inc(o_rstd_ready, 1)

            with pool.Fori(16, 23) as c:
                head_rstd(c)
                past(c + 1)
                head_copy(diff_z, c - 15)
            head_rstd(23)

            pool.wait_ge(gf_loaded, 16)
            for n in range(3):
                sl = slice(n * CHUNK, (n + 1) * CHUNK)
                for m in range(M_TILES):
                    pool.wait_ge(evac[m], 33 + n)
                    pool.tensor_tensor(yg[:, m, sl], y_sb[:, m, sl], rows[:, sl], ALU.mult).then_inc(yg_ready, 1)
            for m in range(M_TILES):
                pool.wait_ge(y_ms_ready, 2 * m + 3)
                pool.tensor_tensor(rstd[:, m:m + 1], ms[:, m:m + 1], neg_half[:, m:m + 1], ALU.pow).then_inc(y_rstd_ready, 1)


def kernel(x, g_norm, w_in, lambda_q1, lambda_k1, lambda_q2, lambda_k2, g_subln, b_forget,
           w_proj_a, w_proj_b, w_out, g_final):
    import concourse.bacc as bacc
    from concourse.bass_utils import run_bass_kernel_spmd

    pos = np.arange(SEQ, dtype=np.float32)
    inv_freq = np.float32(500000.0) ** (-np.arange(ROPE_HALF, dtype=np.float32) * 2.0 / (2 * ROPE_HALF))
    angle = (pos[:, None] * inv_freq[None, :].astype(np.float32)).reshape(M_TILES, P, ROPE_HALF).transpose(1, 0, 2)
    i = np.arange(P)
    consts = np.zeros((P, C_ALL), np.float32)
    consts[:, C_MASK:C_MASK + P] = np.where(i[:, None] >= i[None, :], 0.0, NEG)
    consts[:, C_TRI:C_TRI + P] = i[:, None] <= i[None, :]
    consts[0:2 * HEADS, C_SEL:C_SEL + HEADS] = np.tile(np.eye(HEADS), (2, 1))
    consts[:, C_COS:C_COS + 16] = np.cos(angle).reshape(P, 16)
    consts[:, C_SIN:C_SIN + 16] = np.sin(angle).reshape(P, 16)

    named = dict(x=x, g_norm=g_norm, w_in=w_in, lq1=lambda_q1, lk1=lambda_k1, lq2=lambda_q2, lk2=lambda_k2,
                 g_subln=g_subln, b_forget=b_forget, w_a=w_proj_a, w_b=w_proj_b, w_out=w_out, g_final=g_final,
                 consts=consts)
    nc = bacc.Bacc("TRN2", target_bir_lowering=False, num_devices=1)
    arrays, args = {}, []
    for name, value in named.items():
        a = np.ascontiguousarray(value)
        arrays[f"in_{name}"] = a
        args.append(nc.dram_tensor(f"in_{name}", a.shape, mybir.dt.from_np(a.dtype), kind="ExternalInput").ap())
    args.append(nc.dram_tensor("out_y", (1, SEQ, D_MODEL), mybir.dt.float32, kind="ExternalOutput").ap())
    build(nc, *args)
    r = run_bass_kernel_spmd(nc, [arrays], core_ids=[0])
    return r.results[0]["out_y"]
```
